# Optimizing a Trainium2 kernel written in Bass

```python
import math
import jax, jax.numpy as jnp
from jax import lax
import numpy as np

D_MODEL = 1024
BATCH = 1
SEQ = 512
DEPTH = 1

RMS_EPS = 1e-6
NEG_INF = -1e30

S5_WIDTH = D_MODEL // 2
S5_GROUP = 16
S5_GROUPS = S5_WIDTH // S5_GROUP
S5_STATE = 64

N_Q_HEADS = 16
N_KV_HEADS = 4
HEAD_DIM = 64
Q_PER_KV = N_Q_HEADS // N_KV_HEADS
WINDOW = 128
ATTN_BLOCK = 128
N_BUCKETS = 32
MAX_DISTANCE = 128

PEER_HEADS = 8
PEER_KEY_DIM = 128
N_SUB_KEYS = 128
N_EXPERTS = N_SUB_KEYS * N_SUB_KEYS
PEER_TOPK = 16
PEER_TOKEN_BLOCK = 128

Q_WIDTH = N_Q_HEADS * HEAD_DIM
KV_WIDTH = N_KV_HEADS * HEAD_DIM
GATE_WIDTH = 2 * D_MODEL
IN_WIDTH = S5_WIDTH + Q_WIDTH + 2 * KV_WIDTH + GATE_WIDTH


def rms_norm(x, g):
    xf = x.astype(jnp.float32)
    r = lax.rsqrt(jnp.mean(xf * xf, axis=-1, keepdims=True) + RMS_EPS)
    return (xf * r).astype(x.dtype) * g

def _complex_scan_combine(c1, c2):
    a1r, a1i, b1r, b1i = c1
    a2r, a2i, b2r, b2i = c2
    ar = a2r * a1r - a2i * a1i
    ai = a2r * a1i + a2i * a1r
    br = a2r * b1r - a2i * b1i + b2r
    bi = a2r * b1i + a2i * b1r + b2i
    return (ar, ai, br, bi)

def s5_mixer(u, lam_re, lam_im, log_step, b_re, b_im, c_re, c_im, d_skip, w_glu):
    bsz, seq, _ = u.shape
    f32 = jnp.float32
    uf = u.astype(f32).reshape(bsz, seq, S5_GROUPS, S5_GROUP)
    lr, li = lam_re.astype(f32), lam_im.astype(f32)
    step = jnp.exp(log_step.astype(f32))[:, None]
    mag = jnp.exp(lr * step)
    abar_re = mag * jnp.cos(li * step)
    abar_im = mag * jnp.sin(li * step)
    den = lr * lr + li * li
    nr, ni = abar_re - 1.0, abar_im
    coef_re = ((nr * lr + ni * li) / den)[..., None]
    coef_im = ((ni * lr - nr * li) / den)[..., None]
    br, bi = b_re.astype(f32), b_im.astype(f32)
    bbar_re = coef_re * br - coef_im * bi
    bbar_im = coef_re * bi + coef_im * br
    bu_re = jnp.einsum('blgc,gpc->blgp', uf, bbar_re)
    bu_im = jnp.einsum('blgc,gpc->blgp', uf, bbar_im)
    a_re = jnp.broadcast_to(abar_re, bu_re.shape)
    a_im = jnp.broadcast_to(abar_im, bu_im.shape)
    _, _, h_re, h_im = lax.associative_scan(
        _complex_scan_combine, (a_re, a_im, bu_re, bu_im), axis=1)
    y = (jnp.einsum('blgp,gcp->blgc', h_re, c_re.astype(f32))
         - jnp.einsum('blgp,gcp->blgc', h_im, c_im.astype(f32))
         + d_skip.astype(f32) * uf)
    y = jax.nn.gelu(y.reshape(bsz, seq, S5_WIDTH), approximate=False).astype(u.dtype)
    ab = y @ w_glu
    a, b = jnp.split(ab, 2, axis=-1)
    return a * jax.nn.sigmoid(b)

def t5_bucket(dist):
    max_exact = N_BUCKETS // 2
    d_f = jnp.maximum(dist, 1).astype(jnp.float32)
    large = max_exact + (jnp.log(d_f / max_exact) / math.log(MAX_DISTANCE / max_exact)
                         * (N_BUCKETS - max_exact)).astype(jnp.int32)
    large = jnp.minimum(large, N_BUCKETS - 1)
    return jnp.where(dist < max_exact, dist, large)

def sliding_window_attention(q, k, v, q_norm_g, k_norm_g, rel_bias_table, sinks):
    bsz, seq, _ = q.shape
    nb = seq // ATTN_BLOCK
    q = rms_norm(q.reshape(bsz, seq, N_KV_HEADS, Q_PER_KV, HEAD_DIM), q_norm_g)
    k = rms_norm(k.reshape(bsz, seq, N_KV_HEADS, HEAD_DIM), k_norm_g)
    v = v.reshape(bsz, seq, N_KV_HEADS, HEAD_DIM)
    qb = q.reshape(bsz, nb, ATTN_BLOCK, N_KV_HEADS, Q_PER_KV, HEAD_DIM)

    def band(t):
        pad = jnp.pad(t, ((0, 0), (ATTN_BLOCK, 0), (0, 0), (0, 0)))
        prev = pad[:, :seq].reshape(bsz, nb, ATTN_BLOCK, N_KV_HEADS, HEAD_DIM)
        cur = t.reshape(bsz, nb, ATTN_BLOCK, N_KV_HEADS, HEAD_DIM)
        return jnp.concatenate([prev, cur], axis=2)

    kb, vb = band(k), band(v)
    scale = HEAD_DIM ** -0.5
    scores = jnp.einsum('bnqkgd,bnskd->bnkgqs', qb, kb).astype(jnp.float32) * scale

    qi = jnp.arange(ATTN_BLOCK)[:, None]
    si = jnp.arange(2 * ATTN_BLOCK)[None, :]
    dist = ATTN_BLOCK + qi - si
    band_ok = (dist >= 0) & (dist < WINDOW)
    bias = rel_bias_table.astype(jnp.float32)[t5_bucket(jnp.maximum(dist, 0))]
    bias = bias.transpose(2, 0, 1).reshape(N_KV_HEADS, Q_PER_KV, ATTN_BLOCK, 2 * ATTN_BLOCK)
    blk = jnp.arange(nb)[:, None, None]
    key_ok = (blk - 1) * ATTN_BLOCK + si[None] >= 0
    valid = (band_ok[None] & key_ok)[None, :, None, None]

    scores = jnp.where(valid, scores + bias, NEG_INF)
    sink = sinks.astype(jnp.float32).reshape(1, 1, N_KV_HEADS, Q_PER_KV, 1, 1)
    m = jnp.maximum(jnp.max(scores, axis=-1, keepdims=True), sink)
    p = jnp.exp(scores - m)
    p = p / (jnp.sum(p, axis=-1, keepdims=True) + jnp.exp(sink - m))
    out = jnp.einsum('bnkgqs,bnskd->bnqkgd', p.astype(vb.dtype), vb)
    return out.reshape(bsz, seq, Q_WIDTH)

def peer_mixer(xn, w_query, sub_keys, u_tab, v_tab):
    bsz, seq, d = xn.shape
    t = bsz * seq
    xt = xn.reshape(t, d)
    q = (xt @ w_query).reshape(t, PEER_HEADS, 2, PEER_KEY_DIM // 2)
    s = jnp.einsum('thkd,hknd->thkn', q, sub_keys).astype(jnp.float32)
    vals, idx = lax.top_k(s, PEER_TOPK)
    cand = (vals[:, :, 0, :, None] + vals[:, :, 1, None, :]).reshape(t, PEER_HEADS, PEER_TOPK * PEER_TOPK)
    best, pos = lax.top_k(cand, PEER_TOPK)
    i1 = jnp.take_along_axis(idx[:, :, 0], pos // PEER_TOPK, axis=-1)
    i2 = jnp.take_along_axis(idx[:, :, 1], pos % PEER_TOPK, axis=-1)
    expert = (i1 * N_SUB_KEYS + i2).reshape(t, PEER_HEADS * PEER_TOPK)
    gate = jax.nn.softmax(best, axis=-1).reshape(t, PEER_HEADS * PEER_TOPK)

    def block_fn(args):
        xb, eb, gb = args
        a = jnp.einsum('cd,ced->ce', xb, u_tab[eb]).astype(jnp.float32)
        w = (gb * jax.nn.gelu(a, approximate=False)).astype(xb.dtype)
        return jnp.einsum('ce,ced->cd', w, v_tab[eb])

    nblk = t // PEER_TOKEN_BLOCK
    out = lax.map(block_fn, (xt.reshape(nblk, PEER_TOKEN_BLOCK, d),
                             expert.reshape(nblk, PEER_TOKEN_BLOCK, -1),
                             gate.reshape(nblk, PEER_TOKEN_BLOCK, -1)))
    return out.reshape(bsz, seq, d)

def first_inputs(seed: int = 0) -> dict:
    key = jax.random.key(seed)
    ks = jax.random.split(key, 26)
    f32 = jnp.float32
    L, D, G, P, C = DEPTH, D_MODEL, S5_GROUPS, S5_STATE, S5_GROUP
    nrm = lambda k, shape, s: jax.random.normal(k, shape, f32) * s
    inp = {}
    inp['x'] = nrm(ks[0], (BATCH, SEQ, D), 1.0)
    inp['ln1_g'] = 1.0 + nrm(ks[1], (L, D), 0.02)
    inp['w_in'] = nrm(ks[2], (L, D, IN_WIDTH), D ** -0.5)
    inp['b_gate'] = nrm(ks[3], (L, GATE_WIDTH), 0.02)
    inp['s5_lambda_re'] = -0.5 + nrm(ks[4], (L, G, P), 0.01)
    inp['s5_lambda_im'] = jnp.pi * jnp.arange(P, dtype=f32) + nrm(ks[5], (L, G, P), 0.01)
    inp['s5_log_step'] = jax.random.uniform(ks[6], (L, G), f32, math.log(1e-3), math.log(1e-1))
    inp['s5_b_re'] = nrm(ks[7], (L, G, P, C), (2 * C) ** -0.5)
    inp['s5_b_im'] = nrm(ks[8], (L, G, P, C), (2 * C) ** -0.5)
    inp['s5_c_re'] = nrm(ks[9], (L, G, C, P), P ** -0.5)
    inp['s5_c_im'] = nrm(ks[10], (L, G, C, P), P ** -0.5)
    inp['s5_d'] = nrm(ks[11], (L, G, C), 1.0)
    inp['s5_w_glu'] = nrm(ks[12], (L, S5_WIDTH, 2 * S5_WIDTH), S5_WIDTH ** -0.5)
    inp['w_s5_branch'] = nrm(ks[13], (L, S5_WIDTH, D), S5_WIDTH ** -0.5)
    inp['q_norm_g'] = 1.0 + nrm(ks[14], (L, HEAD_DIM), 0.02)
    inp['k_norm_g'] = 1.0 + nrm(ks[15], (L, HEAD_DIM), 0.02)
    inp['rel_bias_table'] = nrm(ks[16], (N_BUCKETS, N_Q_HEADS), 0.1)
    inp['attn_sinks'] = nrm(ks[17], (L, N_Q_HEADS), 0.5)
    inp['w_attn_branch'] = nrm(ks[18], (L, Q_WIDTH, D), Q_WIDTH ** -0.5)
    inp['w_out'] = nrm(ks[19], (L, D, D), D ** -0.5)
    inp['ln2_g'] = 1.0 + nrm(ks[20], (L, D), 0.02)
    inp['peer_w_query'] = nrm(ks[21], (L, D, PEER_HEADS * PEER_KEY_DIM), D ** -0.5)
    inp['peer_sub_keys'] = nrm(ks[22], (L, PEER_HEADS, 2, N_SUB_KEYS, PEER_KEY_DIM // 2), (PEER_KEY_DIM // 2) ** -0.5)
    inp['peer_u'] = nrm(ks[23], (L, N_EXPERTS, D), D ** -0.5)
    inp['peer_v'] = nrm(ks[24], (L, N_EXPERTS, D), D ** -0.5)
    return inp

def first_block(x, ln1_g, w_in, b_gate, s5_lambda_re, s5_lambda_im, s5_log_step,
              s5_b_re, s5_b_im, s5_c_re, s5_c_im, s5_d, s5_w_glu, w_s5_branch,
              q_norm_g, k_norm_g, rel_bias_table, attn_sinks, w_attn_branch, w_out,
              ln2_g, peer_w_query, peer_sub_keys, peer_u, peer_v):
    splits = [S5_WIDTH, S5_WIDTH + Q_WIDTH, S5_WIDTH + Q_WIDTH + KV_WIDTH,
              S5_WIDTH + Q_WIDTH + 2 * KV_WIDTH]
    h = x
    for layer in range(DEPTH):
        xn = rms_norm(h, ln1_g[layer])
        proj = xn @ w_in[layer]
        u_s5, q, k, v, gate_logits = jnp.split(proj, splits, axis=-1)
        gates = jax.nn.sigmoid(gate_logits + b_gate[layer])
        g_s5, g_attn = jnp.split(gates, 2, axis=-1)
        y_s5 = s5_mixer(u_s5, s5_lambda_re[layer], s5_lambda_im[layer], s5_log_step[layer],
                        s5_b_re[layer], s5_b_im[layer], s5_c_re[layer], s5_c_im[layer],
                        s5_d[layer], s5_w_glu[layer]) @ w_s5_branch[layer]
        y_attn = sliding_window_attention(q, k, v, q_norm_g[layer], k_norm_g[layer],
                                          rel_bias_table, attn_sinks[layer]) @ w_attn_branch[layer]
        h = h + (g_s5 * y_s5 + g_attn * y_attn) @ w_out[layer]
        xn2 = rms_norm(h, ln2_g[layer])
        h = h + peer_mixer(xn2, peer_w_query[layer], peer_sub_keys[layer],
                           peer_u[layer], peer_v[layer])
    return h


D_MIX = D_MODEL
NSA_HEADS = 8
NSA_KV_HEADS = 2
NSA_WIDTH = NSA_HEADS * HEAD_DIM
KV_W = NSA_KV_HEADS * HEAD_DIM
CONV_GROUPS = 8
CONV_WIDTH = D_MIX - NSA_WIDTH
CONV_K = 3
CMP_BLK = 32
CMP_STRIDE = 16
SEL_BLK = 64
SEL_TOPN = 8
WINDOW_2 = 512
Q_BLK = 64
FORCE_SCORE = 1e4
REL_BUCKETS = 32
REL_MAX_DIST = 128
PEER_NKEYS = 128
PEER_EXPERTS = PEER_NKEYS * PEER_NKEYS
PEER_QDIM = 128
PEER_CHUNK = 128
EPS = 1e-6

IN_SIZES = (NSA_WIDTH, KV_W, KV_W, KV_W, KV_W, KV_W, KV_W, NSA_HEADS * 3,
            CONV_WIDTH, CONV_WIDTH, CONV_WIDTH)
IN_COLS = sum(IN_SIZES)
SPLIT_POINTS = tuple(int(v) for v in np.cumsum(IN_SIZES)[:-1])


def rmsnorm(x, g):
    x32 = x.astype(jnp.float32)
    y = x32 * lax.rsqrt(jnp.mean(x32 * x32, axis=-1, keepdims=True) + EPS)
    return y.astype(x.dtype) * g

def masked_softmax(logits, mask):
    logits = jnp.where(mask, logits.astype(jnp.float32), -1e30)
    p = jax.nn.softmax(logits, axis=-1)
    return jnp.where(jnp.any(mask, axis=-1, keepdims=True), p, 0.0)

def rel_bucket(dist):
    n = jnp.maximum(dist, 0)
    exact = REL_BUCKETS // 2
    log_ratio = jnp.log(jnp.maximum(n, 1).astype(jnp.float32) / exact) / math.log(REL_MAX_DIST / exact)
    large = exact + (log_ratio * (REL_BUCKETS - exact)).astype(jnp.int32)
    return jnp.where(n < exact, n, jnp.minimum(large, REL_BUCKETS - 1))

def nsa_mixer(q, kc_tok, vc_tok, ks_tok, vs_tok, kw_tok, vw_tok, gates,
              cmp_pe_k, cmp_pe_v, cmp_wk1, cmp_wk2, cmp_wv1, cmp_wv2, rel_table):
    B, S = q.shape[0], q.shape[1]
    G, R, dh = NSA_KV_HEADS, NSA_HEADS // NSA_KV_HEADS, HEAD_DIM

    n_cmp = (S - CMP_BLK) // CMP_STRIDE + 1
    cmp_start = np.arange(n_cmp) * CMP_STRIDE
    tok_idx = cmp_start[:, None] + np.arange(CMP_BLK)[None, :]
    cmp_end = jnp.asarray(cmp_start + CMP_BLK - 1, jnp.int32)

    def compress(tok, pe, w1, w2):
        blk = tok[:, tok_idx] + pe[None, None, :, None, :]
        flat = blk.transpose(0, 1, 3, 2, 4).reshape(B, n_cmp, G, CMP_BLK * dh)
        return jax.nn.gelu(flat @ w1) @ w2

    kc = compress(kc_tok, cmp_pe_k, cmp_wk1, cmp_wk2)
    vc = compress(vc_tok, cmp_pe_v, cmp_wv1, cmp_wv2)

    n_slc = S // SEL_BLK
    n_sel = min(SEL_TOPN, n_slc)
    slc_start = np.arange(n_slc) * SEL_BLK
    overlap = (cmp_start[:, None] < slc_start[None, :] + SEL_BLK) & (cmp_start[:, None] + CMP_BLK > slc_start[None, :])
    cmp_to_slc = jnp.asarray(overlap, jnp.float32)
    ks_blk = ks_tok.reshape(B, n_slc, SEL_BLK, G, dh).transpose(0, 3, 1, 2, 4)
    vs_blk = vs_tok.reshape(B, n_slc, SEL_BLK, G, dh).transpose(0, 3, 1, 2, 4)

    kw_pad = jnp.pad(kw_tok, ((0, 0), (WINDOW_2, 0), (0, 0), (0, 0)))
    vw_pad = jnp.pad(vw_tok, ((0, 0), (WINDOW_2, 0), (0, 0), (0, 0)))

    b_ix = jnp.arange(B)[:, None, None]
    g_ix = jnp.arange(G)[None, :, None]
    rel_g = rel_table.reshape(REL_BUCKETS, G, R)
    blk_ids = jnp.arange(n_slc)
    scale = HEAD_DIM ** -0.5

    def head_bias(dist):
        return jnp.transpose(rel_table[rel_bucket(dist)], (2, 0, 1)).reshape(G, R, *dist.shape)

    def query_block(i):
        t0 = i * Q_BLK
        t = t0 + jnp.arange(Q_BLK)
        qb = lax.dynamic_slice_in_dim(q, t0, Q_BLK, axis=1).reshape(B, Q_BLK, G, R, dh) * scale
        gb = jax.nn.sigmoid(lax.dynamic_slice_in_dim(gates, t0, Q_BLK, axis=1).astype(jnp.float32))
        gb = gb.reshape(B, Q_BLK, G, R, 3)

        s = jnp.einsum('bqgrd,bngd->bgrqn', qb, kc) + head_bias(t[:, None] - cmp_end[None, :])
        p_cmp = masked_softmax(s, cmp_end[None, :] <= t[:, None])
        o_cmp = jnp.einsum('bgrqn,bngd->bqgrd', p_cmp, vc)

        imp = jnp.einsum('bgrqn,nj->bgqj', p_cmp, cmp_to_slc)
        cur = t // SEL_BLK
        forced = (blk_ids[None, :] == 0) | (blk_ids[None, :] == cur[:, None]) | (blk_ids[None, :] == cur[:, None] - 1)
        allowed = blk_ids[None, :] * SEL_BLK <= t[:, None]
        imp = jnp.where(forced, FORCE_SCORE, jnp.where(allowed, imp, -jnp.inf))
        _, sel = lax.top_k(imp, n_sel)
        L = n_sel * SEL_BLK
        sel_flat = sel.reshape(B, G, Q_BLK * n_sel)
        ks = ks_blk[b_ix, g_ix, sel_flat].reshape(B, G, Q_BLK, L, dh)
        vs = vs_blk[b_ix, g_ix, sel_flat].reshape(B, G, Q_BLK, L, dh)
        kpos = (sel[..., None] * SEL_BLK + jnp.arange(SEL_BLK)).reshape(B, G, Q_BLK, L)
        dist = t[:, None] - kpos
        bias = rel_g[rel_bucket(dist), jnp.arange(G)[:, None, None]]
        s = jnp.einsum('bqgrd,bgqld->bgrql', qb, ks) + bias.transpose(0, 1, 4, 2, 3)
        p = masked_softmax(s, (dist >= 0)[:, :, None])
        o_slc = jnp.einsum('bgrql,bgqld->bqgrd', p, vs)

        kw = lax.dynamic_slice_in_dim(kw_pad, t0, Q_BLK + WINDOW_2, axis=1)
        vw = lax.dynamic_slice_in_dim(vw_pad, t0, Q_BLK + WINDOW_2, axis=1)
        kpos_w = t0 - WINDOW_2 + jnp.arange(Q_BLK + WINDOW_2)
        dist_w = t[:, None] - kpos_w[None, :]
        mask_w = (dist_w >= 0) & (dist_w < WINDOW_2) & (kpos_w[None, :] >= 0)
        s = jnp.einsum('bqgrd,blgd->bgrql', qb, kw) + head_bias(dist_w)
        p = masked_softmax(s, mask_w)
        o_win = jnp.einsum('bgrql,blgd->bqgrd', p, vw)

        o = gb[..., 0:1] * o_cmp + gb[..., 1:2] * o_slc + gb[..., 2:3] * o_win
        return o.reshape(B, Q_BLK, NSA_WIDTH)

    out = lax.map(query_block, jnp.arange(S // Q_BLK))
    return out.transpose(1, 0, 2, 3).reshape(B, S, NSA_WIDTH)

def short_conv_mixer(h, b_gate, c_gate, conv_w):
    z = c_gate * h
    y = lax.conv_general_dilated(z, conv_w.astype(z.dtype), window_strides=(1,),
                                 padding=((CONV_K - 1, 0),),
                                 dimension_numbers=('NWC', 'WIO', 'NWC'),
                                 feature_group_count=CONV_WIDTH)
    return b_gate * y

def peer_ffn(xn, w_q, sub_keys, expert_u, expert_v):
    B, S, D = xn.shape
    q = (xn @ w_q).reshape(B, S, PEER_HEADS, 2, PEER_QDIM // 2)
    s = jnp.einsum('bshpd,hpkd->bshpk', q, sub_keys)
    v_half, i_half = lax.top_k(s, PEER_TOPK)
    cand = v_half[..., 0, :, None] + v_half[..., 1, None, :]
    top_s, top_c = lax.top_k(cand.reshape(B, S, PEER_HEADS, PEER_TOPK * PEER_TOPK), PEER_TOPK)
    i1 = jnp.take_along_axis(i_half[..., 0, :], top_c // PEER_TOPK, axis=-1)
    i2 = jnp.take_along_axis(i_half[..., 1, :], top_c % PEER_TOPK, axis=-1)
    experts = i1 * PEER_NKEYS + i2
    g = jax.nn.softmax(top_s.astype(jnp.float32), axis=-1)
    E = PEER_HEADS * PEER_TOPK
    n_chunk = (B * S) // PEER_CHUNK
    xs = xn.reshape(n_chunk, PEER_CHUNK, D)
    es = experts.reshape(n_chunk, PEER_CHUNK, E)
    gs = g.reshape(n_chunk, PEER_CHUNK, E)

    def chunk(args):
        xc, ec, gc = args
        u = expert_u[ec]
        act = jax.nn.gelu(jnp.einsum('cd,ced->ce', xc, u).astype(jnp.float32))
        return jnp.einsum('ce,ced->cd', gc * act, expert_v[ec])

    return lax.map(chunk, (xs, es, gs)).reshape(B, S, D)

def second_inputs(seed: int = 0) -> dict:
    key = jax.random.key(seed)
    ks = jax.random.split(key, 24)
    L, D, dh = DEPTH, D_MODEL, HEAD_DIM

    def nrm(k, shape, s):
        return jax.random.normal(k, shape, jnp.float32) * s

    def gain(k, shape):
        return 1.0 + 0.05 * jax.random.normal(k, shape, jnp.float32)

    return {
        'x': nrm(ks[0], (BATCH, SEQ, D), 1.0),
        'c': nrm(ks[1], (BATCH, D), 1.0),
        'ln_mix_g': gain(ks[2], (L, D)),
        'ln_ffn_g': gain(ks[3], (L, D)),
        'w_mod': nrm(ks[4], (L, D, 6 * D), 0.5 * D ** -0.5),
        'b_mod': nrm(ks[5], (L, 6 * D), 0.02),
        'w_in': nrm(ks[6], (L, D, IN_COLS), D ** -0.5),
        'cmp_pe_k': nrm(ks[7], (L, CMP_BLK, dh), 0.1),
        'cmp_pe_v': nrm(ks[8], (L, CMP_BLK, dh), 0.1),
        'cmp_wk1': nrm(ks[9], (L, CMP_BLK * dh, dh), (CMP_BLK * dh) ** -0.5),
        'cmp_wk2': nrm(ks[10], (L, dh, dh), dh ** -0.5),
        'cmp_wv1': nrm(ks[11], (L, CMP_BLK * dh, dh), (CMP_BLK * dh) ** -0.5),
        'cmp_wv2': nrm(ks[12], (L, dh, dh), dh ** -0.5),
        'conv_w': nrm(ks[13], (L, CONV_K, 1, CONV_WIDTH), CONV_K ** -0.5),
        'norm_attn_g': gain(ks[14], (L, NSA_WIDTH)),
        'norm_conv_g': gain(ks[15], (L, CONV_WIDTH)),
        'w_out': nrm(ks[16], (L, D_MIX, D), D_MIX ** -0.5),
        'peer_wq': nrm(ks[17], (L, D, PEER_HEADS * PEER_QDIM), D ** -0.5),
        'peer_keys': nrm(ks[18], (L, PEER_HEADS, 2, PEER_NKEYS, PEER_QDIM // 2), (PEER_QDIM // 2) ** -0.5),
        'peer_u': nrm(ks[19], (L, PEER_EXPERTS, D), D ** -0.5),
        'peer_v': nrm(ks[20], (L, PEER_EXPERTS, D), PEER_HEADS ** -0.5),
        'rel_table': nrm(ks[21], (REL_BUCKETS, NSA_HEADS), 0.5),
        'ln_final_g': gain(ks[22], (D,)),
    }

def second_block(x, c, ln_mix_g, ln_ffn_g, w_mod, b_mod, w_in, cmp_pe_k, cmp_pe_v,
              cmp_wk1, cmp_wk2, cmp_wv1, cmp_wv2, conv_w, norm_attn_g, norm_conv_g,
              w_out, peer_wq, peer_keys, peer_u, peer_v, rel_table, ln_final_g):
    B, S = x.shape[0], x.shape[1]
    c_act = jax.nn.silu(c)
    for l in range(DEPTH):
        mod = (c_act @ w_mod[l] + b_mod[l])[:, None, :]
        sh1, sc1, gt1, sh2, sc2, gt2 = jnp.split(mod, 6, axis=-1)

        h = rmsnorm(x, ln_mix_g[l]) * (1 + sc1) + sh1
        proj = h @ w_in[l]
        q, kc, vc, ksl, vsl, kw, vw, gts, cb, cc, ch = jnp.split(proj, SPLIT_POINTS, axis=-1)
        kv = lambda a: a.reshape(B, S, NSA_KV_HEADS, HEAD_DIM)
        o_attn = nsa_mixer(q.reshape(B, S, NSA_HEADS, HEAD_DIM), kv(kc), kv(vc), kv(ksl), kv(vsl),
                           kv(kw), kv(vw), gts.reshape(B, S, NSA_HEADS, 3),
                           cmp_pe_k[l], cmp_pe_v[l], cmp_wk1[l], cmp_wk2[l], cmp_wv1[l], cmp_wv2[l],
                           rel_table)
        o_conv = short_conv_mixer(ch, cb, cc, conv_w[l])
        mixed = jnp.concatenate([rmsnorm(o_attn, norm_attn_g[l]), rmsnorm(o_conv, norm_conv_g[l])], axis=-1)
        x = x + gt1 * (mixed @ w_out[l])

        h2 = rmsnorm(x, ln_ffn_g[l]) * (1 + sc2) + sh2
        x = x + gt2 * peer_ffn(h2, peer_wq[l], peer_keys[l], peer_u[l], peer_v[l])
    return rmsnorm(x, ln_final_g)


def setup_inputs(seed=0):
    out = dict(first_inputs(seed))
    for name, value in second_inputs(seed + 1).items():
        if name != "x":
            out[name + "_2"] = value
    return out


def reference(
    x, ln1_g, w_in, b_gate, s5_lambda_re, s5_lambda_im, s5_log_step, s5_b_re, s5_b_im, s5_c_re,
    s5_c_im, s5_d, s5_w_glu, w_s5_branch, q_norm_g, k_norm_g, rel_bias_table, attn_sinks,
    w_attn_branch, w_out, ln2_g, peer_w_query, peer_sub_keys, peer_u, peer_v, c_2, ln_mix_g_2,
    ln_ffn_g_2, w_mod_2, b_mod_2, w_in_2, cmp_pe_k_2, cmp_pe_v_2, cmp_wk1_2, cmp_wk2_2,
    cmp_wv1_2, cmp_wv2_2, conv_w_2, norm_attn_g_2, norm_conv_g_2, w_out_2, peer_wq_2,
    peer_keys_2, peer_u_2, peer_v_2, rel_table_2, ln_final_g_2,
):
    x = first_block(
        x, ln1_g, w_in, b_gate, s5_lambda_re, s5_lambda_im, s5_log_step, s5_b_re, s5_b_im,
        s5_c_re, s5_c_im, s5_d, s5_w_glu, w_s5_branch, q_norm_g, k_norm_g, rel_bias_table,
        attn_sinks, w_attn_branch, w_out, ln2_g, peer_w_query, peer_sub_keys, peer_u, peer_v,
    )
    return second_block(
        x, c_2, ln_mix_g_2, ln_ffn_g_2, w_mod_2, b_mod_2, w_in_2, cmp_pe_k_2, cmp_pe_v_2,
        cmp_wk1_2, cmp_wk2_2, cmp_wv1_2, cmp_wv2_2, conv_w_2, norm_attn_g_2, norm_conv_g_2,
        w_out_2, peer_wq_2, peer_keys_2, peer_u_2, peer_v_2, rel_table_2, ln_final_g_2,
    )


_drawn_inputs = setup_inputs


def setup_inputs(seed=0):
    import zlib

    import numpy as np

    out = dict(_drawn_inputs(seed))
    spreads = {}
    factors = {'ln1_g': 7.381,
     'b_gate': 8.0,
     's5_lambda_re': 64.0,
     's5_lambda_im': 3.021,
     's5_log_step': 3.048,
     's5_b_re': 4.052,
     's5_b_im': 4.129,
     's5_c_re': 4.071,
     's5_c_im': 4.059,
     'q_norm_g': 8.0,
     'k_norm_g': 8.0,
     'rel_bias_table': 5.583,
     'attn_sinks': 8.0,
     'ln2_g': 8.0,
     'peer_w_query': 3.349,
     'peer_sub_keys': 3.357,
     'peer_u': 3.693,
     'peer_v': 3.346,
     'ln_mix_g_2': 2.737,
     'ln_ffn_g_2': 22.581,
     'cmp_pe_k_2': 29.893,
     'cmp_pe_v_2': 25.86,
     'norm_attn_g_2': 38.182,
     'norm_conv_g_2': 39.208,
     'b_mod_2': 3.212,
     'rel_table_2': 3.02}
    for name, (base, spread) in spreads.items():
        noise = np.random.default_rng([zlib.crc32(name.encode()), seed]).standard_normal(out[name].shape)
        drawn = base * np.exp(spread * noise) if base else spread * noise
        out[name] = __import__('jax').numpy.asarray(drawn.astype(out[name].dtype))
    for name, factor in factors.items():
        out[name] = (out[name] * factor).astype(out[name].dtype)
    return out
```

```python
import math
from contextlib import ExitStack

import numpy as np
import concourse.bass as bass
from concourse import mybir
from concourse.alu_op_type import AluOpType as ALU

ACT = mybir.ActivationFunctionType
F32 = mybir.dt.float32
U32 = mybir.dt.uint32
AXX = mybir.AxisListType.X
NT = 4
NEG = -1e30
D = 1024
W1 = 384
W2 = 640
N_IN1 = 4096
N_IN2 = 2840
RING = 8
NWS = 4


class Eng:

    def __init__(self, e):
        self.e = e
        self.seen = {}
        self.clock = 0.0

    def wait(self, toks):
        for sem, val in toks:
            if self.seen.get(id(sem), 0) < val:
                self.seen[id(sem)] = val
                self.e.wait_ge(sem, val)


class Forecast:

    def __init__(self):
        self.at = {}

    def of(self, toks):
        return max([self.at.get((id(s), v), 0.0) for s, v in toks] + [0.0])

    def put(self, tok, t):
        self.at[(id(tok[0]), tok[1])] = t
        return tok


class Queue:

    def __init__(self, eng, sem, cast, chain=True, weave=None):
        self.eng, self.sem, self.n, self.chain = eng, sem, 0, chain
        self.cast, self.weave = cast, weave

    def __call__(self, fn, *toks, d=0.5):
        if self.chain and self.n:
            toks = toks + ((self.sem, self.n),)
        toks = [t for t in toks if t]
        ready = self.cast.of(toks)
        if self.weave:
            self.weave(self.eng, ready)
        self.eng.wait(toks)
        self.n += 1
        fn(self.eng.e).then_inc(self.sem, 1)
        self.eng.clock = max(self.eng.clock, ready) + d
        return self.cast.put((self.sem, self.n), self.eng.clock + 0.15)

    def now(self):
        return (self.sem, self.n) if self.n else None


class Dma:

    def __init__(self, eng, sem, cast, wire):
        self.eng, self.sem, self.n = eng, sem, 0
        self.cast, self.wire = cast, wire

    def __call__(self, fn, *toks, d=0.3):
        toks = [t for t in toks if t]
        self.eng.wait(toks)
        self.n += 16
        fn(self.eng.e).then_inc(self.sem, 16)
        self.eng.clock = max(self.eng.clock, self.cast.of(toks)) + 0.1
        self.wire[0] = max(self.wire[0], self.eng.clock) + d
        return self.cast.put((self.sem, self.n), self.wire[0] + 2.0)


def build(nc, A, out, act_counts):
    ctx = ExitStack()
    with ctx:
        total = [0]

        def sb(name, shape, dt=F32):
            return ctx.enter_context(nc.sbuf_tensor(name, shape, dt))

        nsem = [0]

        def sem(name):
            nsem[0] += 1
            return ctx.enter_context(nc.semaphore(name))

        ps_all = ctx.enter_context(nc.psum_tensor("ps", [128, 8, 512], F32))
        PS = [ps_all[:, i, :] for i in range(8)]
        PA = PS[6:8]

        vec, sca, ten, pool, syn = Eng(nc.vector), Eng(nc.scalar), Eng(nc.tensor), Eng(nc.gpsimd), Eng(nc.sync)
        cast = Forecast()
        wire = [0.0]
        pend = [None, None]

        def g_next():
            pend[1] = next(pend[0], None)
            if pend[1] is None:
                pend[0] = None

        def g_start():
            if pend[0] is None:
                return 1e30
            eng, when = pend[1]
            if eng is None:
                return 1e30 if route_done[when] is None else 0.0
            return max(eng.clock, when)

        def weave(eng, ready):
            while g_start() <= max(eng.clock, ready):
                g_next()

        def gathered(n):
            while gather_done[n] is None:
                assert g_start() < 1e30
                g_next()
            return gather_done[n]

        V = Queue(vec, sem("vA"), cast, weave=weave)
        S = Queue(sca, sem("sA"), cast, weave=weave)
        T = Queue(ten, sem("tA"), cast, chain=False, weave=weave)
        VG = Queue(vec, sem("vG"), cast, chain=False)
        SG = Queue(sca, sem("sG"), cast, chain=False)
        TG = Queue(ten, sem("tG"), cast, chain=False)

        def dma(name):
            return Dma(syn, sem("d_" + name), cast, wire)

        ident = sb("ident", [128, 128])
        shm = sb("shm", [128, 4, 128])
        iot = sb("iot", [128, 16])
        rmask = sb("rmask", [128, 1])
        hres = sb("hres", [128, NT, D])
        ring = sb("ring", [128, RING, D])
        xn = sb("xn", [128, 2, D])
        idx = sb("idx", [128, 2, 128], U32)
        gate = sb("gate", [128, 2, 128])
        aw = sb("aw", [128, 2, 128])
        diag = sb("diag", [128, 4, 128])
        wsl = sb("wsl", [128, NWS, 4, 512])
        xr = sb("xr", [128, D])
        xT = sb("xT", [128, 8, 128])
        st = sb("st", [128, 8])
        cols = sb("cols", [128, 64])
        skT = sb("skT", [128, 8, 128])
        rowA = sb("rowA", [128, D])
        rowB = sb("rowB", [128, D])
        big = sb("big", [128, 6144 + 384])
        pers = sb("pers", [128, 13312])

        def carve(base, start, *shape, dt=F32):
            n = int(np.prod(shape))
            ap = base[:, start:start + n]
            if dt != F32:
                ap = ap.bitcast(dt)
            if len(shape) == 2:
                ap = ap.rearrange("p (a b) -> p a b", b=shape[1])
            if len(shape) == 3:
                ap = ap.rearrange("p (a b c) -> p a b c", b=shape[1], c=shape[2])
            return ap, start + n

        def bc(ap, shape):
            return ap.broadcast_to(shape)

        L1d = nc.dram_tensor("L1d", [16, 128, W1], F32, kind="Internal").ap()
        L2d = nc.dram_tensor("L2d", [8, 128, W2], F32, kind="Internal").ap()

        d_c = [dma(f"c{i}") for i in range(40)]
        nload = [0]

        def load(dst, src, *toks):
            q = d_c[nload[0]]
            nload[0] += 1
            return q(lambda e: e.dma_start(dst, src), *toks)

        t_id = load(ident[:, :], A["k_ident"])
        t_x = [load(hres[:, i, :], A["x"][0, 128 * i:128 * i + 128, :]) for i in range(NT)]
        t_cols = load(cols[:, 0:54], A["k_cols"])
        t_shm = load(shm[:, :, :], A["k_shift"])
        t_iot = load(iot[:, :], A["k_iota"])
        t_rm = load(rmask[:, :], A["k_rmask"])
        g1c = cols[:, 0:8]
        qgc, kgc, dcol = cols[:, 8:9], cols[:, 9:10], cols[:, 10:14]
        lnm, ngc, ccol = cols[:, 16:24], cols[:, 24:32], cols[:, 32:40]

        w_dma = [dma(f"w{i}") for i in range(NWS)]
        w_free = [None] * NWS
        w_n = [0]
        w_out = [0]

        def w_load(w, k0, kc, c0, n):
            s = w_n[0] % NWS
            w_n[0] += 1
            w_out[0] += 1
            assert w_out[0] <= NWS
            src = w[k0 * 128:(k0 + kc) * 128, c0:c0 + n].rearrange("(k p) n -> p k n", p=128)
            t = w_dma[s](lambda e: e.dma_start(wsl[:, s, 0:kc, 0:n], src), w_free[s], d=n / 512 * 2.9)
            return s, t

        bank_free = {}

        class Proj:

            def __init__(self, w, nk, blocks):
                self.w, self.nk = w, nk
                self.blocks = blocks
                self.units = [(b, k0) for b in range(len(blocks)) for k0 in range(0, nk, 4)]
                self.at = 0
                self.got = {}

            def ahead(self, n):
                while self.at < len(self.units) and self.at < n:
                    b, k0 = self.units[self.at]
                    c0, w = self.blocks[b]
                    self.got[self.at] = w_load(self.w, k0, 4, c0, w)
                    self.at += 1

            def run(self, lhsT, t_l, evac, banks):
                per = self.nk // 4
                for b, (c0, n) in enumerate(self.blocks):
                    bank = banks[b % len(banks)]
                    for u in range(per):
                        i = b * per + u
                        self.ahead(i + 1)
                        s, t_w = self.got[i]

                        def f(e, s=s, u=u, bank=bank, n=n):
                            for k in range(4):
                                kk = 4 * u + k
                                r = e.matmul(PS[bank][:, 0:n], lhsT(kk), wsl[:, s, k, 0:n],
                                             start=(kk == 0), stop=(kk == self.nk - 1))
                            return r
                        t_mm = T(f, t_w, t_l, bank_free.get(bank), d=4 * 0.86 * n / 512)
                        w_out[0] -= 1
                        w_free[s] = t_mm
                        self.ahead(i + 1 + NWS)
                        yield 1
                    bank_free[bank] = evac(b, PS[bank], t_mm)
                    yield 1

        def rstd(src, t_src, n, c):
            t = S(lambda e: e.activation(xr[:, 0:n], src, ACT.Square, accum_out=st[:, c:c + 1]), t_src, V.now(), T.now())
            t = V(lambda e: e.tensor_scalar(st[:, c:c + 1], st[:, c:c + 1], 1.0 / n, 1e-6, ALU.mult, ALU.add), t)
            t = V(lambda e: e.reciprocal(st[:, c:c + 1], st[:, c:c + 1]), t)
            return S(lambda e: e.activation(st[:, c:c + 1], st[:, c:c + 1], ACT.Sqrt), t)

        def turn(srcs, t_src, bank, t_bank, rows=128):
            def f(e):
                for j, s in enumerate(srcs):
                    r = e.transpose(PS[bank][:, j * 128:(j + 1) * 128], s, ident[:, :])
                return r
            return T(f, t_src, t_bank, t_id)

        def P3(bank, n=4):
            return PS[bank][:, :].rearrange("p (a b) -> p a b", a=n)

        def turn8(src, t_src, dst, evac, t_dst=None):
            toks = []
            for hh in range(2):
                t = turn([src(4 * hh + j) for j in range(4)], t_src, hh, V.now())
                toks.append(t)
            for hh in range(2):
                t = evac(hh, P3(hh), toks[hh], t_dst)
            return t

        def scale_evac(g):
            def f(hh, ps, t, t_dst):
                return V(lambda e: e.tensor_tensor(xT[:, 4 * hh:4 * hh + 4, :], ps,
                                                   bc(g[:, 4 * hh:4 * hh + 4].unsqueeze(2), [128, 4, 128]),
                                                   ALU.mult), t, t_cols, T.now())
            return f

        def copy_evac(dst):
            def f(hh, ps, t, t_dst):
                return V(lambda e: e.tensor_copy(dst[:, 4 * hh:4 * hh + 4, :], ps), t, t_dst)
            return f

        o = 0
        Ec, o = carve(pers, o, 16, 128)
        Es, o = carve(pers, o, 16, 128)
        bias1, o = carve(pers, o, 16, 256)
        kT1, o = carve(pers, o, 2, 512)
        v1, o = carve(pers, o, 2, 256)
        BT, o = carve(pers, o, 8, 128)
        CT, o = carve(pers, o, 32, 32)
        hst, o = carve(pers, o, 2, 16)
        magc, o = carve(pers, o, 16)
        snk, o = carve(pers, o, 16)
        assert o <= 13312, o

        def size(ap):
            return int(np.prod(ap.shape[1:]))

        def tt(out, a, b, op, *toks):
            return V(lambda e: e.tensor_tensor(out, a, b, op), *toks, d=0.1 + size(out) / 960)

        def ts(out, a, s1, s2, o1, o2, *toks):
            if s2 is None:
                return V(lambda e: e.tensor_scalar(out, a, s1, None, o1), *toks, d=0.1 + size(out) / 960)
            return V(lambda e: e.tensor_scalar(out, a, s1, s2, o1, o2), *toks, d=0.1 + size(out) / 960)

        def act(out, a, f, *toks, **kw):
            return S(lambda e: e.activation(out, a, f, **kw), *toks, d=0.3 + size(out) / 1200)

        t_C = [None]
        t_bias = [None]

        def make_bias(tab, nh, oh, msk, w, Ld, dst, keys, t_dst):
            o = 0
            ohb, o = carve(big, o, w)
            mk, o = carve(big, o, w)
            tb, o = carve(big, o, 16)
            lv, o = carve(big, o, w)
            t1 = load(ohb[0:32, :], oh, V.now(), T.now(), S.now())
            t2 = load(mk[0:nh, :], msk)
            t3 = load(tb[0:32, 0:nh], tab)
            a = min(512, w)

            def f(e):
                r = e.matmul(PS[0][0:nh, 0:a], tb[0:32, 0:nh], ohb[0:32, 0:a], start=True, stop=True)
                if w > 512:
                    r = e.matmul(PS[1][0:nh, 0:w - 512], tb[0:32, 0:nh], ohb[0:32, 512:w], start=True, stop=True)
                return r
            t = T(f, t1, t3, V.now())
            t = tt(lv[0:nh, 0:a], PS[0][0:nh, 0:a], mk[0:nh, 0:a], ALU.add, t, t2)
            if w > 512:
                t = tt(lv[0:nh, 512:w], PS[1][0:nh, 0:w - 512], mk[0:nh, 512:w], ALU.add)
            t = load(Ld, bc(lv[0:nh, 0:w].unsqueeze(1), [nh, 128, w]), t)
            src = bass.AP(tensor=Ld.tensor, offset=127, ap=[[w - 1, 128], [128 * w, nh], [1, keys]])
            return load(dst, src, t, t_dst)

        def setup1():
            lc = st
            o = 0
            prm, o = carve(big, o, 4, 16)
            tmp, o = carve(big, o, 12, 16)
            craw, o = carve(big, o, 32, 32)
            ctm, o = carve(big, o, 32, 32)
            ea, o = carve(big, o, 16, 64)
            t_p = load(prm[:, :, :], A["k_s5p"])
            t_b = load(BT[:, :, :], A["k_s5b"])
            t_cr = load(craw[:, :, :], A["k_s5c"])
            t_s = load(snk[:, :], A["attn_sinks"].broadcast_to([128, 16]))
            lr, li, ls = prm[:, 0, :], prm[:, 1, :], prm[:, 2, :]
            step, th, w0, w1, w2, w3 = [tmp[:, i, :] for i in range(6)]
            cs, sn, cr, ci, den = [tmp[:, i, :] for i in range(6, 11)]
            t = act(step, ls, ACT.Exp, t_p)
            t = tt(th, li, step, ALU.mult, t)
            t = tt(w0, lr, step, ALU.mult)
            t = act(magc[:, :], w0, ACT.Exp, t)
            C1 = 6.28125
            C2 = float(np.float32(2 * math.pi - C1))
            C3 = 2 * math.pi - C1 - C2
            for dst, turn_ in ((sn, 0.0), (cs, 0.25)):
                ts(w1, th, 1.0 / (2 * math.pi), turn_, ALU.mult, ALU.add)
                ts(w1, w1, 12582912.0, None, ALU.add, None)
                ts(w1, w1, -12582912.0, None, ALU.add, None)
                V(lambda e: e.scalar_tensor_tensor(w2, w1, -C1, th, ALU.mult, ALU.add), t)
                V(lambda e: e.scalar_tensor_tensor(w2, w1, -C2, w2, ALU.mult, ALU.add))
                V(lambda e: e.scalar_tensor_tensor(w2, w1, -C3, w2, ALU.mult, ALU.add))
                if turn_:
                    ts(w2, w2, math.pi / 2, None, ALU.add, None)
                t = ts(w2, w2, 3.1415925, -3.1415925, ALU.min, ALU.max)
                t = act(dst, w2, ACT.Sin, t)
            tt(w0, magc[:, :], cs, ALU.mult, t)
            ts(w0, w0, -1.0, None, ALU.add, None)
            tt(w1, magc[:, :], sn, ALU.mult)
            tt(den, lr, lr, ALU.mult)
            tt(w2, li, li, ALU.mult)
            tt(den, den, w2, ALU.add)
            V(lambda e: e.reciprocal(den, den))
            tt(cr, w0, lr, ALU.mult)
            tt(w2, w1, li, ALU.mult)
            tt(cr, cr, w2, ALU.add)
            tt(cr, cr, den, ALU.mult)
            tt(ci, w1, lr, ALU.mult)
            tt(w2, w0, li, ALU.mult)
            tt(ci, ci, w2, ALU.subtract)
            t = tt(ci, ci, den, ALU.mult)
            yield 1
            crb = bc(cr.unsqueeze(2), [128, 16, 32])
            cib = bc(ci.unsqueeze(2), [128, 16, 32])
            t = tt(CT[:, 0:16, :], craw[:, 0:16, :], crb, ALU.mult, t_cr)
            tt(ctm[:, 0:16, :], craw[:, 16:32, :], cib, ALU.mult)
            tt(CT[:, 0:16, :], CT[:, 0:16, :], ctm[:, 0:16, :], ALU.subtract)
            tt(CT[:, 16:32, :], craw[:, 0:16, :], cib, ALU.mult)
            tt(ctm[:, 0:16, :], craw[:, 16:32, :], crb, ALU.mult)
            tt(CT[:, 16:32, :], CT[:, 16:32, :], ctm[:, 0:16, :], ALU.add)
            ts(CT[:, 16:32, :], CT[:, 16:32, :], -1.0, None, ALU.mult, None)
            V(lambda e: e.tensor_copy(Ec[:, :, 0:1], cs.unsqueeze(2)))
            V(lambda e: e.tensor_copy(Es[:, :, 0:1], sn.unsqueeze(2)))
            n = 1
            while n < 128:
                ac = bc(Ec[:, :, n - 1:n], [128, 16, n])
                as_ = bc(Es[:, :, n - 1:n], [128, 16, n])
                tt(ea[:, :, 0:n], Es[:, :, 0:n], as_, ALU.mult)
                tt(Ec[:, :, n:2 * n], Ec[:, :, 0:n], ac, ALU.mult)
                tt(Ec[:, :, n:2 * n], Ec[:, :, n:2 * n], ea[:, :, 0:n], ALU.subtract)
                tt(ea[:, :, 0:n], Es[:, :, 0:n], ac, ALU.mult)
                tt(Es[:, :, n:2 * n], Ec[:, :, 0:n], as_, ALU.mult)
                tt(Es[:, :, n:2 * n], Es[:, :, n:2 * n], ea[:, :, 0:n], ALU.add)
                n *= 2
                yield 1
            t_C[0] = V(lambda e: e.memset(hst[:, :, :], 0.0), t_b, t_s)
            t_bias[0] = make_bias(A["rel_bias_table"], 16, A["k_oh1"], A["k_mask1"], W1, L1d,
                                  bias1[:, :, :], 256, None)

        HB = [0, 256]

        def block1(i):
            W = A["w_in"][0]
            pin = Proj(W, 8, [(512 * b, 512) for b in range(8)])
            pin.ahead(NWS)
            o = 0
            gt, o = carve(big, o, 2048)
            mix, o = carve(big, o, 1024)
            o0 = o
            uT, o = carve(big, o, 4, 128)
            qs, o = carve(big, o, 1024)
            kk, o = carve(big, o, 256)
            t_r = rstd(hres[:, i, :], t_x[i], D, 0)
            t = ts(xr[:, :], hres[:, i, :], st[:, 0:1], None, ALU.mult, None, t_r)
            t_xT = turn8(lambda k: xr[:, k * 128:(k + 1) * 128], t, xT, scale_evac(g1c))
            yield 1
            bg = [None]
            t_bg = load1(gt, A["b_gate"][0].unsqueeze(0).broadcast_to([128, 2048]), V.now(), S.now(), T.now())
            last = {}

            def evac(b, ps, t):
                if b == 0:
                    r = act(xr[:, 0:512], ps[:, :], ACT.Copy, t, V.now())
                elif b < 3:
                    r = act(qs[:, 512 * (b - 1):512 * b], ps[:, :], ACT.Copy, t, V.now(), T.now())
                elif b == 3:
                    act(kk[:, :], ps[:, 0:256], ACT.Copy, t, V.now())
                    r = act(v1[:, i % 2, :], ps[:, 256:512], ACT.Copy, V.now(), T.now())
                else:
                    g = gt[:, 512 * (b - 4):512 * (b - 3)]
                    r = tt(g, ps[:, :], g, ALU.add, t, t_bg)
                    act(g, g, ACT.Sigmoid, r)
                last[b] = r
                return r
            yield from pin.run(lambda k: xT[:, k, :], t_xT, evac, [4, 5])
            pg = Proj(A["s5_w_glu"][0], 4, [(0, 512), (512, 512)])
            pg.ahead(2)
            t_gates = S.now()
            t = turn([xr[:, j * 128:(j + 1) * 128] for j in range(4)], last[0], 0, V.now())
            t_uT = V(lambda e: e.tensor_copy(uT[:, :, :], P3(0)), t)
            sq, _ = carve(big, o, 1024)
            q3 = qs.rearrange("p (h d) -> p h d", d=64)
            k3 = kk.rearrange("p (h d) -> p h d", d=64)
            hn = cols2
            t = act(sq[:, :], qs[:, :], ACT.Square, V.now())
            t = V(lambda e: e.tensor_reduce(hn[:, 0:16], sq.rearrange("p (h d) -> p h d", d=64), AXX, ALU.add), t)
            t = act(sq[:, 0:256], kk[:, :], ACT.Square, t)
            V(lambda e: e.tensor_reduce(hn[:, 16:20], sq[:, 0:256].rearrange("p (h d) -> p h d", d=64), AXX, ALU.add), t)
            ts(hn[:, 0:20], hn[:, 0:20], 1.0 / 64, 1e-6, ALU.mult, ALU.add)
            t = V(lambda e: e.reciprocal(hn[:, 0:20], hn[:, 0:20]))
            t = act(hn[:, 0:20], hn[:, 0:20], ACT.Sqrt, t)
            tt(q3, q3, bc(hn[:, 0:16].unsqueeze(2), [128, 16, 64]), ALU.mult, t)
            t = tt(k3, k3, bc(hn[:, 16:20].unsqueeze(2), [128, 4, 64]), ALU.mult)
            yield 1
            q4 = qs.rearrange("p (m a r d) -> p m r a d", m=2, a=2, r=4)
            V(lambda e: e.tensor_copy(sq.rearrange("p (m r a d) -> p m r a d", m=2, r=4, a=2)[:, 0], q4[:, 0]))
            t = V(lambda e: e.tensor_copy(sq.rearrange("p (m r a d) -> p m r a d", m=2, r=4, a=2)[:, 1], q4[:, 1]))
            for hh in range(2):
                t = turn([sq[:, 512 * hh + j * 128:512 * hh + (j + 1) * 128] for j in range(4)], V.now(), hh, V.now())
                t = ts(xT[:, 4 * hh:4 * hh + 4, :], P3(hh), qgc, 0.125, ALU.mult, ALU.mult, t)
            t_qT = t
            t = turn([kk[:, 0:128], kk[:, 128:256]], V.now(), 0, V.now())
            t_kT = ts(kT1[:, :, 128 * i:128 * i + 128], PS[0][:, 0:256].rearrange("p (a b) -> p a b", a=2), kgc,
                      None, ALU.mult, None, t)
            yield 1
            o = o0 + 512
            sc, o = carve(big, o, 4, 256)
            PT, o = carve(big, o, 4, 256)
            assert o <= 6528, o
            av = xr
            s0 = 128 if i == 0 else 0
            mx = cols2[:, 20:36]
            nm = cols2[:, 36:52]
            sm = cols2[:, 52:68]
            t_sc_free = t_pt_free = None
            for g in range(4):
                m, a = g // 2, g % 2

                def f(e, m=m, a=a):
                    for r in range(4):
                        b = r // 2
                        k0 = 128 * (i - 1) + s0
                        x = e.matmul(PS[b][:, 256 * (r % 2) + s0:256 * (r % 2) + 256],
                                     xT[64 * a:64 * a + 64, 4 * m + r, :],
                                     kT1[64 * a:64 * a + 64, m, k0:128 * (i + 1)], start=True, stop=True)
                    return x
                t = T(f, t_qT, t_kT, V.now(), S.now())
                for b in range(2):
                    t = tt(sc[:, 2 * b:2 * b + 2, s0:256], PS[b][:, :].rearrange("p (a b) -> p a b", a=2)[:, :, s0:256],
                           bias1[:, 4 * g + 2 * b:4 * g + 2 * b + 2, s0:256], ALU.add, t, t_bias[0], T.now())
                V(lambda e: e.tensor_reduce(mx[:, 4 * g:4 * g + 4], sc[:, :, s0:256], AXX, ALU.max))
                tt(mx[:, 4 * g:4 * g + 4], mx[:, 4 * g:4 * g + 4], snk[:, 4 * g:4 * g + 4], ALU.max)
                t = ts(nm[:, 4 * g:4 * g + 4], mx[:, 4 * g:4 * g + 4], -1.0, None, ALU.mult, None)
                for r in range(4):
                    h = 4 * g + r
                    t = act(sc[:, r, s0:256], sc[:, r, s0:256], ACT.Exp, t, bias=nm[:, h:h + 1],
                            accum_out=sm[:, h:h + 1])
                yield 1
                for b in range(2):
                    def f(e, b=b):
                        for r in range(2):
                            for k in range(s0 // 128, 2):
                                x = e.transpose(PS[2 + b][:, 256 * r + 128 * k:256 * r + 128 * k + 128],
                                                sc[:, 2 * b + r, 128 * k:128 * k + 128], ident[:, :])
                        return x
                    t_t = T(f, t, V.now(), S.now())
                    w = V if b else S
                    src = PS[2 + b][:, :].rearrange("p (a b) -> p a b", a=2)[:, :, s0:256]
                    dst = PT[:, 2 * b:2 * b + 2, s0:256]
                    if b:
                        t_p1 = V(lambda e, src=src, dst=dst: e.tensor_copy(dst, src), t_t)
                    else:
                        t_p0 = act(dst, src, ACT.Copy, t_t, T.now())

                def f(e, g=g):
                    for r in range(4):
                        h = 4 * g + r
                        ks = range(s0 // 128, 2)
                        for k in ks:
                            x = e.matmul(PS[4 + h // 8][:, 64 * (h % 8):64 * (h % 8) + 64],
                                         PT[:, r, 128 * k:128 * k + 128],
                                         v1[:, (i + 1 + k) % 2, 64 * g:64 * g + 64],
                                         start=(k == ks[0]), stop=(k == 1))
                    return x
                t_pv = T(f, t_p0, t_p1, V.now())
                yield 1
            tt(mx, snk[:, :], mx, ALU.subtract)
            t = act(mx, mx, ACT.Exp, V.now())
            tt(sm, sm, mx, ALU.add, t)
            V(lambda e: e.reciprocal(sm, sm))
            for b in range(2):
                t = tt(av[:, 512 * b:512 * b + 512].rearrange("p (h d) -> p h d", d=64),
                       PS[4 + b][:, :].rearrange("p (h d) -> p h d", d=64),
                       bc(sm[:, 8 * b:8 * b + 8].unsqueeze(2), [128, 8, 64]), ALU.mult, t_pv)
            yield 1
            pa = Proj(A["w_attn_branch"][0], 8, [(0, 512), (512, 512)])
            t_xT = turn8(lambda k: av[:, k * 128:(k + 1) * 128], t, xT, copy_evac(xT[:, :, :]), t_pv)

            def evac(b, ps, t):
                return tt(mix[:, 512 * b:512 * b + 512], ps[:, :], gt[:, 1024 + 512 * b:1536 + 512 * b], ALU.mult,
                          t, t_gates)
            t_attn_x = t_xT
            o = o0 + 512
            b0, o = carve(big, o, 4, 128)
            b1, o = carve(big, o, 4, 128)
            b2, o = carve(big, o, 4, 128)
            b3, o = carve(big, o, 4, 128)
            yT = carve(big, o, 4, 128)[0]
            t_y = None
            for c in range(4):
                def f(e, c=c):
                    for z in range(2):
                        for j in range(4):
                            x = e.matmul(PS[j][:, 128 * z:128 * z + 128], BT[32 * j:32 * j + 32, 4 * z + c, :],
                                         uT[32 * j:32 * j + 32, c, :], start=True, stop=True,
                                         tile_position=(32 * j, 0))
                    return x
                t = T(f, t_uT, t_C[0], V.now())
                ec, es = Ec[:, 4 * c:4 * c + 4, :], Es[:, 4 * c:4 * c + 4, :]
                pr, pi = ps_all[:, 0:4, 0:128], ps_all[:, 0:4, 128:256]
                tt(b0, pr, ec, ALU.mult, t, T.now())
                tt(b1, pi, es, ALU.mult)
                tt(b0, b0, b1, ALU.add)
                tt(b1, pi, ec, ALU.mult)
                tt(b2, pr, es, ALU.mult)
                tt(b1, b1, b2, ALU.subtract)
                yield 1
                for j in range(4):
                    jj = 4 * c + j
                    for z, bb, dd in ((0, b0, b2), (1, b1, b3)):
                        V(lambda e, jj=jj, z=z, bb=bb, dd=dd, j=j: e.tensor_tensor_scan(
                            dd[:, j, :], bc(magc[:, jj:jj + 1], [128, 128]), bb[:, j, :], hst[:, z, jj:jj + 1],
                            ALU.mult, ALU.add))
                yield 1
                tt(b0, b2, ec, ALU.mult)
                tt(b1, b3, es, ALU.mult)
                tt(b0, b0, b1, ALU.subtract)
                tt(b1, b3, ec, ALU.mult)
                tt(b2, b2, es, ALU.mult)
                tt(b1, b1, b2, ALU.add)
                V(lambda e, c=c: e.tensor_copy(hst[:, 0, 4 * c:4 * c + 4].unsqueeze(2), b0[:, :, 127:128]))
                t = V(lambda e, c=c: e.tensor_copy(hst[:, 1, 4 * c:4 * c + 4].unsqueeze(2), b1[:, :, 127:128]))

                def f(e, c=c):
                    for j in range(4):
                        for z, bb in ((0, b0), (1, b1)):
                            x = e.matmul(PS[4][32 * j:32 * j + 32, 128 * c:128 * c + 128],
                                         CT[:, 16 * z + 4 * c + j, :], bb[:, j, :], start=(z == 0), stop=(z == 1),
                                         tile_position=(0, 32 * j))
                    return x
                t = T(f, t)
                V(lambda e, c=c: e.scalar_tensor_tensor(yT[:, c, :], uT[:, c, :], dcol[:, c:c + 1],
                                                        PS[4][:, 128 * c:128 * c + 128], ALU.mult, ALU.add),
                  t, t_cols)
                yield 1
            t = act(yT, yT, ACT.Gelu, V.now())
            gl = b0

            def evac_glu(b, ps, t):
                if b == 0:
                    return V(lambda e: e.tensor_copy(qa, ps[:, :]), t)
                r = act(qb, ps[:, :], ACT.Sigmoid, t, V.now())
                tt(qa, qa, qb, ALU.mult, r)
                return r
            qa = b0.rearrange("p a b -> p (a b)")
            qb = b1.rearrange("p a b -> p (a b)")
            yield from pg.run(lambda k: yT[:, k, :], t, evac_glu, [4, 5])
            pa.ahead(2)
            yield from pa.run(lambda k: xT[:, k, :], t_attn_x, evac, [4, 5])
            ps_ = Proj(A["w_s5_branch"][0], 4, [(0, 512), (512, 512)])
            ps_.ahead(2)
            t = turn([qa[:, j * 128:(j + 1) * 128] for j in range(4)], V.now(), 0, V.now())
            t = V(lambda e: e.tensor_copy(yT, P3(0)), t)

            def evac_s(b, ps, t):
                g = gt[:, 512 * b:512 * b + 512]
                r = tt(g, ps[:, :], g, ALU.mult, t)
                tt(mix[:, 512 * b:512 * b + 512], mix[:, 512 * b:512 * b + 512], g, ALU.add)
                return r
            yield from ps_.run(lambda k: yT[:, k, :], t, evac_s, [4, 5])
            po = Proj(A["w_out"][0], 8, [(0, 512), (512, 512)])
            po.ahead(NWS)
            t = turn8(lambda k: mix[:, k * 128:(k + 1) * 128], V.now(), xT, copy_evac(xT[:, :, :]), T.now())

            def evac_o(b, ps, t):
                h = hres[:, i, 512 * b:512 * b + 512]
                return tt(h, ps[:, :], h, ALU.add, t)
            yield from po.run(lambda k: xT[:, k, :], t, evac_o, [4, 5])

        d_bg = dma("bg")

        def load1(dst, src, *toks):
            return d_bg(lambda e: e.dma_start(dst, src), *toks)

        cols2 = sb("cols2", [128, 96])

        route_done = [None] * 8
        gather_done = [None] * 8

        t_rows = [None, None]

        def route(n, t_h):
            i, blk, b = n % 4, n // 4, n % 2
            wq = A["peer_w_query"][0] if blk == 0 else A["peer_wq_2"][0]
            pq = Proj(wq, 8, [(0, 512), (512, 512)])
            pq.ahead(NWS)
            o = 0
            sS, o = carve(big, o, 16, 128)
            s2, o = carve(big, o, 256)
            vals, o = carve(big, o, 16, 16)
            ixu, o = carve(big, o, 16, 16, dt=U32)
            ixf, o = carve(big, o, 16, 16)
            best, o = carve(big, o, 8, 16)
            pos, o = carve(big, o, 8, 16, dt=U32)
            pi_, o = carve(big, o, 8, 16, dt=U32)
            pf, o = carve(big, o, 8, 16)
            e1, o = carve(big, o, 8, 16)
            e2, o = carve(big, o, 8, 16)
            oh, o = carve(big, o, 16, 16)
            cand = sS.rearrange("p a b -> p (a b)").rearrange("p (h c) -> p h c", h=8)
            free = gathered(n - 2) if n >= 2 else ()
            t_r = rstd(hres[:, i, :], t_h, D, 1)
            X = xn[:, b, :]
            t = V(lambda e: e.scalar_tensor_tensor(X, hres[:, i, :], st[:, 1:2], rowA[:, :], ALU.mult, ALU.mult),
                  t_r, t_rows[0], *free)
            if blk:
                t = tt(X, X, rowB[:, :], ALU.add, t_rows[1])
            t = turn8(lambda k: X[:, k * 128:(k + 1) * 128], t, xT, copy_evac(xT[:, :, :]), T.now())
            yield 1

            def evac(bb, ps, t):
                return act(xr[:, 512 * bb:512 * bb + 512], ps[:, :], ACT.Copy, t, V.now())
            yield from pq.run(lambda k: xT[:, k, :], t, evac, [4, 5])
            t = turn8(lambda k: xr[:, k * 128:(k + 1) * 128], S.now(), xT, copy_evac(xT[:, :, :]), T.now())
            yield 1
            def f(e):
                for h in range(8):
                    for k in range(2):
                        x = e.matmul(PS[2 * k + h // 4][:, 128 * (h % 4):128 * (h % 4) + 128],
                                     xT[64 * k:64 * k + 64, h, :], skT[64 * k:64 * k + 64, h, :],
                                     start=True, stop=True, tile_position=(64 * k, 0))
                return x
            t2 = T(f, t, t_sk[blk], V.now(), S.now())
            sS4 = sS.rearrange("p (h k) c -> p h k c", k=2)
            for p in range(4):
                act(sS4[:, 4 * (p % 2):4 * (p % 2) + 4, p // 2, :], P3(p), ACT.Copy, t2, V.now())
            t = S.now()
            yield 1

            def top16(src, scratch, vd, idd):
                V(lambda e: e.max(vd[:, 0:8], src))
                V(lambda e: e.max_index(idd[:, 0:8], vd[:, 0:8], src))
                V(lambda e: e.match_replace(scratch, vd[:, 0:8], src, -3.0e38))
                V(lambda e: e.max(vd[:, 8:16], scratch))
                V(lambda e: e.max_index(idd[:, 8:16], vd[:, 8:16], scratch))
            vec.wait([t])
            for g in range(16):
                top16(sS[:, g, :], s2[:, 0:128], vals[:, g, :], ixu[:, g, :])
                yield 1
            V(lambda e: e.tensor_copy(ixf, ixu))
            v4 = vals.rearrange("p (h k) c -> p h k c", k=2)
            c4 = cand.rearrange("p h (a b) -> p h a b", a=16)
            for h0 in range(8):
                tt(c4[:, h0], bc(v4[:, h0, 0, :].unsqueeze(2), [128, 16, 16]),
                   bc(v4[:, h0, 1, :].unsqueeze(1), [128, 16, 16]), ALU.add)
            yield 1
            for h in range(8):
                top16(cand[:, h, :], s2[:, :], best[:, h, :], pos[:, h, :])
                yield 1
            i4 = ixf.rearrange("p (h k) c -> p h k c", k=2)
            for k, dst in ((0, e1), (1, e2)):
                if k == 0:
                    ts(pi_, pos, 4, None, ALU.logical_shift_right, None)
                else:
                    ts(pi_, pos, 15, None, ALU.bitwise_and, None)
                V(lambda e: e.tensor_copy(pf, pi_))
                for h in range(8):
                    tt(oh, bc(pf[:, h, :].unsqueeze(2), [128, 16, 16]), bc(iot[:, :].unsqueeze(1), [128, 16, 16]),
                       ALU.is_equal, t_iot)
                    tt(oh, oh, bc(i4[:, h, k, :].unsqueeze(1), [128, 16, 16]), ALU.mult)
                    V(lambda e, h=h, dst=dst: e.tensor_reduce(dst[:, h, :], oh, AXX, ALU.add))
                    if h % 4 == 3:
                        yield 1
            V(lambda e: e.scalar_tensor_tensor(e1, e1, 128.0, e2, ALU.mult, ALU.add))
            V(lambda e: e.tensor_copy(idx[:, b, :].rearrange("p (h c) -> p h c", h=8), e1), *free)
            V(lambda e: e.tensor_copy(e1[:, :, 0:1], best[:, :, 0:1]))
            tt(best, best, bc(e1[:, :, 0:1], [128, 8, 16]), ALU.subtract)
            t = act(best, best, ACT.Exp, V.now())
            V(lambda e: e.tensor_reduce(e2[:, :, 0:1], best, AXX, ALU.add), t)
            V(lambda e: e.reciprocal(e2[:, :, 0:1], e2[:, :, 0:1]))
            route_done[n] = tt(gate[:, b, :].rearrange("p (h c) -> p h c", h=8), best,
                               bc(e2[:, :, 0:1], [128, 8, 16]), ALU.mult)

        t_sk = [None, None]
        r_sem = [sem(f"ring{i}") for i in range(RING)]
        r_cnt = [0] * RING
        r_free = [None] * RING
        r_n = [0]

        def fetch(tab, n, e_):
            s = r_n[0] % RING
            r_n[0] += 1
            r_cnt[s] += 16
            toks = [x for x in (r_free[s], route_done[n]) if x]
            pool.wait(toks)
            ix = idx[:, n % 2, e_:e_ + 1]
            pool.e.indirect_dma_start(out=ring[:, s, :], out_offset=None, in_=tab,
                                      in_offset=bass.IndirectOffsetOnAxis(ap=ix, axis=0)).then_inc(r_sem[s], 16)
            pool.clock = max(pool.clock, cast.of(toks)) + 1.0
            wire[0] = max(wire[0], pool.clock) + 1.5
            return s, cast.put((r_sem[s], r_cnt[s]), wire[0] + 2.0)

        t_w = {}
        dg_n = [0]
        dg_free = [None] * 4
        acc_free = [None]

        def half_u(m, e_):
            n, g = divmod(m, 8)
            b = n % 2
            tab = A["peer_u"][0] if n < 4 else A["peer_u_2"][0]
            k = 16 * g + e_
            s, t = fetch(tab, n, k)
            yield vec, cast.of([t])
            r_free[s] = VG(lambda e: e.tensor_tensor_reduce(ring[:, s, :], ring[:, s, :], xn[:, b, :], 1.0, 0.0,
                                                            ALU.mult, ALU.add, aw[:, b, k:k + 1]), t,
                           gather_done[n - 2][0] if n >= 2 else None, d=1.2)
            if e_ == 15:
                sl = aw[:, b, 16 * g:16 * g + 16]
                tu = r_free[s]
                yield sca, cast.of([tu])
                t = SG(lambda e: e.activation(sl, sl, ACT.Gelu if n < 4 else ACT.Gelu_apprx_tanh), tu, d=0.4)
                yield vec, cast.of([t])
                t_w[m] = VG(lambda e: e.tensor_tensor(sl, sl, gate[:, b, 16 * g:16 * g + 16], ALU.mult), t, d=0.2)

        def half_v(m, e_):
            n, g = divmod(m, 8)
            b = n % 2
            tab = A["peer_v"][0] if n < 4 else A["peer_v_2"][0]
            k = 16 * g + e_
            s, t = fetch(tab, n, k)
            q = dg_n[0] % 4
            dg_n[0] += 1
            yield sca, cast.of([x for x in (t_w[m], dg_free[q]) if x])
            t_d = SG(lambda e: e.activation(diag[:, q, :], ident[:, :], ACT.Copy, scale=aw[:, b, k:k + 1]),
                     t_w[m], dg_free[q], t_id, d=0.4)
            yield ten, cast.of([t, t_d])

            def f(e):
                for c in range(2):
                    r = e.matmul(PA[c][:, :], diag[:, q, :], ring[:, s, 512 * c:512 * c + 512],
                                 start=(k == 0), stop=(k == 127))
                return r
            dg_free[q] = r_free[s] = TG(f, t, t_d, acc_free[0] if k == 0 else None, d=1.75)

        fin = sb("fin", [128, D])
        t_res = [None] * 4
        out_done = []
        out_dma = [Dma(sca, sem(f"o{i}"), cast, wire) for i in range(4)]

        def finish(n):
            i = n % 4
            t = TG.now()
            if n < 4:
                for c in range(2):
                    h = hres[:, i, 512 * c:512 * c + 512]
                    yield vec, cast.of([t])
                    t = VG(lambda e: e.tensor_tensor(h, PA[c][:, :], h, ALU.add), t, d=0.7)
                t_res[i] = acc_free[0] = t
            else:
                for c in range(2):
                    f = fin[:, 512 * c:512 * c + 512]
                    yield vec, cast.of([t])
                    t = VG(lambda e: e.tensor_tensor(f, PA[c][:, :], gt2[:, 512 * c:512 * c + 512], ALU.mult),
                           t, out_done[-1] if out_done else None, d=0.7)
                acc_free[0] = t
                t = VG(lambda e: e.tensor_tensor(fin[:, :], fin[:, :], hres[:, i, :], ALU.add), t, d=1.2)
                yield sca, cast.of([t])
                t = SG(lambda e: e.activation(hres[:, i, :], fin[:, :], ACT.Square, accum_out=st[:, 2:3]), t, d=1.2)
                yield vec, cast.of([t])
                t = VG(lambda e: e.tensor_scalar(st[:, 2:3], st[:, 2:3], 1.0 / D, 1e-6, ALU.mult, ALU.add), t, d=0.1)
                t = VG(lambda e: e.reciprocal(st[:, 2:3], st[:, 2:3]), t, d=0.1)
                yield sca, cast.of([t])
                t = SG(lambda e: e.activation(st[:, 2:3], st[:, 2:3], ACT.Sqrt), t, d=0.3)
                yield vec, cast.of([t])
                t = VG(lambda e: e.scalar_tensor_tensor(fin[:, :], fin[:, :], st[:, 2:3], finr[:, :], ALU.mult,
                                                        ALU.mult), t, d=1.2)
                yield sca, cast.of([t])
                out_done.append(out_dma[i](lambda e: e.dma_start(out[0, 128 * i:128 * i + 128, :], fin[:, :]), t))

        def gathers():
            yield None, 0
            for e_ in range(16):
                yield from half_u(0, e_)
            for m in range(64):
                n = m // 8
                go = m + 1 < 64 and ((m + 1) % 8 != 0 or route_done[n + 1] is not None)
                for e_ in range(16):
                    if go:
                        yield from half_u(m + 1, e_)
                    yield from half_v(m, e_)
                if m % 8 == 7:
                    gather_done[n] = (TG.now(), VG.now(), SG.now())
                    yield from finish(n)
                if not go and m + 1 < 64:
                    yield None, n + 1
                    for e_ in range(16):
                        yield from half_u(m + 1, e_)

        o = 0
        bias2, o = carve(pers, o, 8, 512)
        w1k, o = carve(pers, o, 32, 64)
        w1v, o = carve(pers, o, 32, 64)
        w2k, o = carve(pers, o, 64)
        w2v, o = carve(pers, o, 64)
        pek, o = carve(pers, o, 32)
        pev, o = carve(pers, o, 32)
        kcT, o = carve(pers, o, 512)
        vcT, o = carve(pers, o, 512)
        ksT, o = carve(pers, o, 2, 512)
        vsn, o = carve(pers, o, 4, 256)
        kcc, o = carve(pers, o, 32)
        hv, o = carve(pers, o, 32)
        zprev, o = carve(pers, o, 512)
        gt1, o = carve(pers, o, 1024)
        g1m, o = carve(pers, o, 8)
        sh1, o = carve(pers, o, 8)
        assert o <= 13312, o
        gt2 = sb("gt2", [128, D])
        finr = sb("finr", [128, D])
        t_m2 = [None]
        cwd = [None]

        def setup2():
            V0, T0, S0 = V.now(), T.now(), S.now()
            t = load(w1k, A["k_w1k"], V0, T0, S0)
            toks = [t]
            toks.append(load(w1v, A["k_w1v"]))
            toks.append(load(w2k, A["k_w2k"]))
            toks.append(load(w2v, A["k_w2v"]))
            toks.append(load(pek, A["k_pek"]))
            toks.append(load(pev, A["k_pev"]))
            toks.append(load(finr[:, :], A["ln_final_g_2"].unsqueeze(0).broadcast_to([128, D])))
            t_lf = load(rowA[:, :], A["ln_ffn_g_2"].broadcast_to([128, D]))
            t_sk[1] = load(skT[:, :, :], A["k_sk2"])
            V(lambda e: e.memset(hv, 0.0), V0, T0, S0)
            o = 0
            cb, o = carve(big, o, 8, 128)
            bm, o = carve(big, o, 2, 512)
            rows = {}
            for nm_ in ("sh1", "sc1", "sc2"):
                rows[nm_], o = carve(big, o, 1024)
            ca = st
            t = act(ca[:, :], ccol, ACT.Sigmoid, V.now(), t_cols)
            tt(ca[:, :], ca[:, :], ccol, ALU.mult, t)
            t_cb = V(lambda e: e.tensor_copy(cb, bc(ca[:, :].unsqueeze(2), [128, 8, 128])), T0, S0)
            dst = [rows["sh1"], rows["sc1"], gt1, rowB[:, :], rows["sc2"], gt2[:, :]]
            pm = Proj(A["w_mod_2"][0], 8, [(512 * b, 512) for b in range(12)])
            pm.ahead(NWS)
            bmd = [dma("bm0"), dma("bm1")]
            bmt = {}

            def bload(b):
                bmt[b] = bmd[b % 2](lambda e: e.dma_start(
                    bm[:, b % 2, :], A["b_mod_2"][0:1, 512 * b:512 * b + 512].broadcast_to([128, 512])),
                    V.now(), T0, S0)
            bload(0)
            bload(1)

            def evac(b, ps, t):
                d = dst[b // 2][:, 512 * (b % 2):512 * (b % 2) + 512]
                r = tt(d, ps[:, :], bm[:, b % 2, :], ALU.add, t, bmt[b])
                if b + 2 < 12:
                    bload(b + 2)
                return r
            yield from pm.run(lambda k: cb[:, k, :], t_cb, evac, [4, 5])
            ex = cols2
            for nm_, d, c0 in (("sh1", sh1, 0), ("sc1", g1m, 8)):
                for k in range(8):
                    V(lambda e, nm_=nm_, d=d, k=k: e.tensor_tensor_reduce(
                        xr[:, 0:128], rows[nm_][:, 128 * k:128 * k + 128], ident[:, :], 1.0, 0.0, ALU.mult, ALU.add,
                        d[:, k:k + 1]), T0, S0, S.now())
            V(lambda e: e.scalar_tensor_tensor(g1m, g1m, 1.0, lnm, ALU.add, ALU.mult))
            t_rows[0] = V(lambda e: e.scalar_tensor_tensor(rowA[:, :], rows["sc2"], 1.0, rowA[:, :], ALU.add, ALU.mult),
                          t_lf)
            t_rows[1] = t_rows[0]
            yield 1
            t_bias[0] = make_bias(A["rel_table_2"], 8, A["k_oh2"], A["k_mask2"], W2, L2d, bias2, 512, None)
            t_m2[0] = toks

        def block2(i):
            W = A["w_in_2"][0]
            blocks = [(0, 512), (512, 512), (1024, 280), (1816, 512), (2328, 512), (1304, 512)]
            pin = Proj(W, 8, blocks)
            pin.ahead(NWS)
            o = 0
            o1, o = carve(big, o, 512)
            cm, o = carve(big, o, 512)
            bk, o = carve(big, o, 512)
            q2, o = carve(big, o, 512)
            zz, o = carve(big, o, 512)
            o0 = o
            kwv, o = carve(big, o, 288)
            cw, o = carve(big, o, 3, 512)
            nc_ = 8 * i + 7
            t_cw = load1(cw, A["conv_w_2"][0, :, 0, :].unsqueeze(0).broadcast_to([128, 3, 512]),
                         V.now(), S.now(), T.now())
            t_r = rstd(hres[:, i, :], t_res[i], D, 0)
            t = ts(xr[:, :], hres[:, i, :], st[:, 0:1], None, ALU.mult, None, t_r)

            def ev(hh, ps, t, t_dst):
                for j in range(4):
                    k = 4 * hh + j
                    r = ts(xT[:, k, :], ps[:, j, :], g1m[:, k:k + 1], sh1[:, k:k + 1], ALU.mult, ALU.add, t, T.now())
                return r
            t_xT = turn8(lambda k: xr[:, k * 128:(k + 1) * 128], t, xT, ev)
            yield 1
            gg = cols2[:, 0:24]

            def evac(b, ps, t):
                if b == 0:
                    return V(lambda e: e.tensor_copy(
                        q2.rearrange("p (r g d) -> p g r d", g=2, d=64),
                        ps[:, :].rearrange("p (g r d) -> p g r d", g=2, r=4)), t)
                if b == 1:
                    return act(bk, ps[:, :], ACT.Copy, t, V.now())
                if b == 2:
                    act(kwv[:, 0:256], ps[:, 0:256], ACT.Copy, t, V.now())
                    return act(gg, ps[:, 256:280], ACT.Sigmoid)
                if b == 3:
                    return V(lambda e: e.tensor_copy(zz, ps[:, :]), t, T.now())
                if b == 4:
                    return tt(zz, zz, ps[:, :], ALU.mult, t)
                return act(cm, ps[:, :], ACT.Copy, t, V.now())
            yield from pin.run(lambda k: xT[:, k, :], t_xT, evac, [4, 5])
            t_in = S.now()
            def f(e):
                for sh in range(2):
                    r = e.matmul(PS[sh][:, :], shm[:, sh, :], zz, start=True, stop=(i == 0))
                    if i:
                        r = e.matmul(PS[sh][:, :], shm[:, 2 + sh, :], zprev, start=False, stop=True)
                return r
            t = T(f, V.now(), S.now(), t_shm)
            c1, _ = carve(big, o, 512)
            tt(c1, zz, cw[:, 2, :], ALU.mult, t_cw, T.now())
            V(lambda e: e.tensor_copy(zprev, zz), t)
            tt(zz, PS[0][:, :], cw[:, 1, :], ALU.mult, t)
            tt(c1, c1, zz, ALU.add)
            tt(zz, PS[1][:, :], cw[:, 0, :], ALU.mult)
            tt(c1, c1, zz, ALU.add)
            tt(cm, cm, c1, ALU.mult, t_in)
            yield 1
            t = turn([q2[:, 128 * r:128 * r + 128] for r in range(4)], V.now(), 0, V.now())
            t_qT = ts(xT[:, 0:4, :], P3(0), 0.125, None, ALU.mult, None, t, T.now())
            t = turn([bk[:, 0:128], bk[:, 128:256], bk[:, 256:384], kwv[:, 0:128]], t_in, 1, V.now())
            sl = slice(128 * i, 128 * i + 128)
            V(lambda e: e.tensor_copy(kcT[:, sl], PS[1][:, 0:128]), t)
            V(lambda e: e.tensor_copy(vcT[:, sl], PS[1][:, 128:256]))
            t_kT = V(lambda e: e.tensor_copy(ksT[:, :, sl], PS[1][:, 256:512].rearrange("p (a b) -> p a b", a=2)))
            act(vsn[:, i, 0:128], bk[:, 384:512], ACT.Copy)
            t_vs = act(vsn[:, i, 128:256], kwv[:, 128:256], ACT.Copy)
            yield 1
            n0 = 0 if i == 0 else 8 * i - 1
            nn = nc_ - n0
            o = o0
            blk_, o = carve(big, o, 32, 8)
            hk, o = carve(big, o, 32)
            pc, o = carve(big, o, 8, 32)
            vbd, o = carve(big, o, 2, 256)
            ptc, o = carve(big, o, 2, 128)
            for src, pe_, w1_, w2_, isk in ((kcT, pek, w1k, w2k, True), (vcT, pev, w1v, w2v, False)):
                win = bass.AP(tensor=src.tensor, offset=src.offset + 16 * n0,
                              ap=[list(src.ap[0]), [1, 32], [16, nn]])
                t = tt(blk_[:, :, 0:nn], win, bc(pe_.unsqueeze(2), [128, 32, nn]), ALU.add, *t_m2[0], T.now(), S.now())

                def f(e, w1_=w1_):
                    for g in range(2):
                        for j in range(32):
                            r = e.matmul(PS[2][64 * g:64 * g + 64, 0:nn], w1_[64 * g:64 * g + 64, j, :],
                                         blk_[64 * g:64 * g + 64, j, 0:nn], start=(j == 0), stop=(j == 31),
                                         tile_position=(64 * g, 64 * g))
                    return r
                t = T(f, t, V.now())
                d = hk if isk else hv
                d = hk[:, 0:nn] if isk else hv[:, n0:nc_]
                t = act(d, PS[2][:, 0:nn], ACT.Gelu_apprx_tanh, t, T.now(), V.now())
                if isk:
                    def f(e):
                        for g in range(2):
                            r = e.matmul(PS[3][64 * g:64 * g + 64, 0:nn], w2k[64 * g:64 * g + 64, :],
                                         hk[64 * g:64 * g + 64, 0:nn], start=True, stop=True,
                                         tile_position=(64 * g, 64 * g))
                        return r
                    t = T(f, t, V.now())
                    t_kc = V(lambda e: e.tensor_copy(kcc[:, n0:nc_], PS[3][:, 0:nn]), t)
                else:
                    hv4 = cols2[:, 24:28]

                    def f(e):
                        for g in range(2):
                            for r_ in range(4):
                                r = e.matmul(PS[2 + g][32 * r_:32 * r_ + 32, 128:192],
                                             hv[64 * g:64 * g + 64, :], w2v[64 * g:64 * g + 64, :],
                                             start=True, stop=True, tile_position=(64 * g, 32 * r_))
                        return r
                    t = T(f, t, V.now())
                    V(lambda e: e.memset(vbd, 0.0), T.now())
                    for g in range(2):
                        for r_ in range(4):
                            t = V(lambda e, g=g, r_=r_: e.tensor_copy(
                                vbd[32 * r_:32 * r_ + 32, g, 64 * r_:64 * r_ + 64],
                                PS[2 + g][32 * r_:32 * r_ + 32, 128:192]), t)
                    t_vc = t
                yield 1
            sm = cols2[:, 28:52]
            mx = cols2[:, 52:60]
            def f(e):
                for h in range(8):
                    g, r_ = h // 4, h % 4
                    r = e.matmul(PS[2 + g][:, 32 * r_:32 * r_ + nc_], xT[64 * g:64 * g + 64, r_, :],
                                 kcc[64 * g:64 * g + 64, 0:nc_], start=True, stop=True, tile_position=(64 * g, 0))
                return r
            t = T(f, t_qT, t_kc, V.now())
            V(lambda e: e.memset(pc, 0.0), T.now())
            u0 = 415 - 128 * i
            pcv = pc[:, :, 0:nc_]
            for g in range(2):
                bcm = bass.AP(tensor=bias2.tensor, offset=bias2.offset + u0 + 2048 * g,
                              ap=[list(bias2.ap[0]), [512, 4], [16, nc_]])
                tt(pcv[:, 4 * g:4 * g + 4, :], PS[2 + g][:, 0:128].rearrange("p (a b) -> p a b", a=4)[:, :, 0:nc_],
                   bcm, ALU.add, t, t_bias[0])
            V(lambda e: e.tensor_reduce(mx, pcv, AXX, ALU.max))
            t = tt(pcv, pcv, bc(mx.unsqueeze(2), [128, 8, nc_]), ALU.subtract)
            t = act(pcv, pcv, ACT.Exp, t)
            V(lambda e: e.tensor_reduce(sm[:, 0:8], pcv, AXX, ALU.add), t)
            if i == 0:
                ts(pcv, pcv, rmask[:, 0:1], None, ALU.mult, None, t_rm)
            t = turn([pc.rearrange("p a b -> p (a b)")[:, 128 * g:128 * g + 128] for g in range(2)], V.now(), 3, V.now())
            t = V(lambda e: e.tensor_copy(ptc, PS[3][:, 0:256].rearrange("p (a b) -> p a b", a=2)), t)

            def f(e):
                for g in range(2):
                    r = e.matmul(PS[2][:, 256 * g:256 * g + 256], ptc[:, g, :], vbd[:, g, :], start=True, stop=True)
                return r
            t_oc = T(f, t, t_vc, V.now())
            V(lambda e: e.reciprocal(sm[:, 0:8], sm[:, 0:8]))
            g3 = gg.rearrange("p (h c) -> p h c", c=3)
            tt(sm[:, 0:8], sm[:, 0:8], g3[:, :, 0], ALU.mult, t_in)
            o3 = o1.rearrange("p (h d) -> p h d", d=64)
            tt(o3, PS[2][:, :].rearrange("p (h d) -> p h d", d=64), bc(sm[:, 0:8].unsqueeze(2), [128, 8, 64]),
               ALU.mult, t_oc)
            yield 1
            o = o0
            sc, o = carve(big, o, 2, 512)
            PT, o = carve(big, o, 2, 512)
            tmp, o = carve(big, o, 512)
            assert o <= 6528, o
            Wk = 128 * (i + 1)
            nm = cols2[:, 60:76]
            for br in range(2):
                for h in range(8):
                    g, r_, c = h // 4, h % 4, 8 * br + h
                    hb = h % 2

                    def f(e, g=g, r_=r_, br=br, hb=hb):
                        return e.matmul(PS[hb][:, 0:Wk], xT[64 * g:64 * g + 64, r_, :],
                                        ksT[64 * g:64 * g + 64, br, 0:Wk], start=True, stop=True,
                                        tile_position=(64 * g, 0))
                    t = T(f, t_qT, t_kT, V.now())
                    tt(sc[:, hb, 0:Wk], PS[hb][:, 0:Wk], bias2[:, h, 384 - 128 * i:512], ALU.add, t, T.now(), t_bias[0])
                    t = V(lambda e, c=c, hb=hb: e.tensor_reduce(nm[:, c:c + 1], sc[:, hb, 0:Wk], AXX, ALU.max))
                    t = ts(nm[:, c:c + 1], nm[:, c:c + 1], -1.0, None, ALU.mult, None)
                    t = act(sc[:, hb, 0:Wk], sc[:, hb, 0:Wk], ACT.Exp, t, bias=nm[:, c:c + 1],
                            accum_out=sm[:, 8 + c:9 + c])
                    t = turn([sc[:, hb, 128 * k:128 * k + 128] for k in range(i + 1)], t, 2 + hb, V.now())
                    t = V(lambda e, hb=hb: e.tensor_copy(PT[:, hb, 0:Wk], PS[2 + hb][:, 0:Wk]), t)

                    def f(e, g=g, h=h, br=br, hb=hb):
                        for k in range(i + 1):
                            r = e.matmul(PS[4 + br][:, 64 * h:64 * h + 64], PT[:, hb, 128 * k:128 * k + 128],
                                         vsn[:, k, 128 * br + 64 * g:128 * br + 64 * g + 64],
                                         start=(k == 0), stop=(k == i))
                        return r
                    t_pv = T(f, t, t_vs)
                    yield 1
                V(lambda e, br=br: e.reciprocal(sm[:, 8 + 8 * br:16 + 8 * br], sm[:, 8 + 8 * br:16 + 8 * br]), S.now())
                tt(sm[:, 8 + 8 * br:16 + 8 * br], sm[:, 8 + 8 * br:16 + 8 * br], g3[:, :, 1 + br], ALU.mult)
                t3 = tmp.rearrange("p (h d) -> p h d", d=64)
                tt(t3, PS[4 + br][:, :].rearrange("p (h d) -> p h d", d=64),
                   bc(sm[:, 8 + 8 * br:16 + 8 * br].unsqueeze(2), [128, 8, 64]), ALU.mult, t_pv)
                tt(o1, o1, tmp, ALU.add)
            po = Proj(A["w_out_2"][0], 8, [(0, 512), (512, 512)])
            po.ahead(NWS)
            t = rstd(o1, V.now(), 512, 3)
            t = ts(xr[:, 0:512], o1, st[:, 3:4], None, ALU.mult, None, t)
            t = act(xr[:, 512:1024], cm, ACT.Square, t, T.now(), accum_out=st[:, 4:5])
            ts(st[:, 4:5], st[:, 4:5], 1.0 / 512, 1e-6, ALU.mult, ALU.add, t)
            t = V(lambda e: e.reciprocal(st[:, 4:5], st[:, 4:5]))
            t = act(st[:, 4:5], st[:, 4:5], ACT.Sqrt, t)
            t = ts(xr[:, 512:1024], cm, st[:, 4:5], None, ALU.mult, None, t)
            t = turn8(lambda k: xr[:, k * 128:(k + 1) * 128], t, xT, scale_evac(ngc))
            yield 1

            def evac_o(b, ps, t):
                h = hres[:, i, 512 * b:512 * b + 512]
                r = tt(xr[:, 512 * b:512 * b + 512], ps[:, :], gt1[:, 512 * b:512 * b + 512], ALU.mult, t, T.now())
                tt(h, h, xr[:, 512 * b:512 * b + 512], ALU.add)
                return r
            yield from po.run(lambda k: xT[:, k, :], t, evac_o, [4, 5])

        t_sk[0] = load(skT[:, :, :], A["k_sk1"])
        t_rows[0] = load(rowA[:, :], A["ln2_g"].broadcast_to([128, D]))

        def part(n):
            if n == 0:
                yield from setup1()
            if n == 4:
                yield from setup2()
            if n < 4:
                yield from block1(n)
                yield from route(n, V.now())
            else:
                gathered(n - 4)
                while t_res[n - 4] is None:
                    g_next()
                yield from block2(n - 4)
                yield from route(n, V.now())

        pend[0] = gathers()
        g_next()
        for n in range(8):
            for _ in part(n):
                pass
        while pend[0] is not None:
            g_next()
        sca.wait(out_done)
        syn.wait(out_done)


def _bucket(dist):
    d = np.maximum(dist, 1).astype(np.float32)
    large = 16 + (np.log(d / 16) / math.log(8) * 16).astype(np.int32)
    return np.where(dist < 16, np.maximum(dist, 0), np.minimum(large, 31))


def _constants():
    c = {"k_ident": np.eye(128, dtype=np.float32)}
    sh = np.zeros((128, 4, 128), np.float32)
    for t in range(128):
        for k, back in enumerate((1, 2)):
            if t >= back:
                sh[t - back, k, t] = 1
            else:
                sh[128 + t - back, 2 + k, t] = 1
    c["k_shift"] = sh
    c["k_iota"] = np.tile(np.arange(16, dtype=np.float32), (128, 1))
    c["k_rmask"] = (np.arange(128) >= 31).astype(np.float32)[:, None]
    for nm, w, nh, top, lim in (("1", W1, 16, 255, 128), ("2", W2, 8, 511, 512)):
        dist = top - np.arange(w)
        ok = (dist >= 0) & (dist < lim)
        oh = np.zeros((32, w), np.float32)
        oh[_bucket(dist)[ok], np.arange(w)[ok]] = 1
        c["k_oh" + nm] = oh
        c["k_mask" + nm] = np.tile(np.where(ok, 0, NEG).astype(np.float32), (nh, 1))
    return c


def kernel(**inputs):
    import concourse.bacc as _bacc
    from concourse.bass_utils import run_bass_kernel_spmd as _run

    nc = _bacc.Bacc("TRN2", target_bir_lowering=False, num_devices=1)
    I = {k: np.asarray(v) for k, v in inputs.items()}
    arr = _constants()
    for k in ("x", "w_in", "b_gate", "s5_w_glu", "w_s5_branch", "rel_bias_table", "attn_sinks", "w_attn_branch",
              "w_out", "ln2_g", "peer_w_query", "peer_u", "peer_v", "ln_ffn_g_2", "w_mod_2", "b_mod_2", "w_in_2",
              "conv_w_2", "w_out_2", "peer_wq_2", "peer_u_2", "peer_v_2", "rel_table_2", "ln_final_g_2"):
        arr[k] = I[k]

    def col(v):
        return v.reshape(-1, 128).T
    cols = np.zeros((128, 54), np.float32)
    cols[:, 0:8] = col(I["ln1_g"][0])
    cols[:, 8] = np.tile(I["q_norm_g"][0], 2)
    cols[:, 9] = np.tile(I["k_norm_g"][0], 2)
    cols[:, 10:14] = col(I["s5_d"][0].reshape(512))
    cols[:, 16:24] = col(I["ln_mix_g_2"][0])
    cols[:, 24:28] = col(I["norm_attn_g_2"][0])
    cols[:, 28:32] = col(I["norm_conv_g_2"][0])
    cols[:, 32:40] = col(I["c_2"][0])
    arr["k_cols"] = cols
    p = np.zeros((128, 4, 16), np.float32)
    p[:, 0] = I["s5_lambda_re"][0].reshape(16, 128).T
    p[:, 1] = I["s5_lambda_im"][0].reshape(16, 128).T
    p[:, 2] = np.repeat(I["s5_log_step"][0], 64).reshape(16, 128).T
    arr["k_s5p"] = p
    bt = np.zeros((4, 2, 16, 2, 4, 2, 64), np.float32)
    for z, k in enumerate(("s5_b_re", "s5_b_im")):
        b = I[k][0].reshape(4, 4, 2, 64, 16)
        for g in range(2):
            bt[:, g, :, z, :, g, :] = b[:, :, g].transpose(1, 3, 0, 2)
    arr["k_s5b"] = bt.reshape(128, 8, 128)
    ct = np.zeros((2, 64, 2, 16, 2, 16), np.float32)
    for z, k in enumerate(("s5_c_re", "s5_c_im")):
        b = I[k][0].reshape(16, 2, 16, 64)
        for g in range(2):
            ct[g, :, z, :, g, :] = b[:, g].transpose(2, 0, 1)
    arr["k_s5c"] = ct.reshape(128, 32, 32)
    for nm, k in (("k_sk1", "peer_sub_keys"), ("k_sk2", "peer_keys_2")):
        arr[nm] = I[k][0].transpose(1, 3, 0, 2).reshape(128, 8, 128)
    for nm, k in (("k_w1k", "cmp_wk1_2"), ("k_w1v", "cmp_wv1_2")):
        w = I[k][0].reshape(32, 64, 64).transpose(1, 0, 2)
        arr[nm] = np.concatenate([w, w], 0)
    for nm, k in (("k_w2k", "cmp_wk2_2"), ("k_w2v", "cmp_wv2_2")):
        arr[nm] = np.concatenate([I[k][0]] * 2, 0)
    for nm, k in (("k_pek", "cmp_pe_k_2"), ("k_pev", "cmp_pe_v_2")):
        arr[nm] = np.concatenate([I[k][0].T] * 2, 0)
    A, maps = {}, {}
    for k, a in arr.items():
        a = np.ascontiguousarray(a)
        maps["in_" + k] = a
        A[k] = nc.dram_tensor("in_" + k, a.shape, mybir.dt.from_np(a.dtype), kind="ExternalInput").ap()
    out = nc.dram_tensor("out_0", (1, 512, D), F32, kind="ExternalOutput").ap()
    build(nc, A, out, None)
    r = _run(nc, [maps], core_ids=[0])
    return r.results[0]["out_0"]
```

```python
import math
from contextlib import ExitStack

import numpy as np
import concourse.bass as bass
from concourse import mybir
from concourse.alu_op_type import AluOpType as ALU

ACT = mybir.ActivationFunctionType
F32 = mybir.dt.float32
U32 = mybir.dt.uint32
AXX = mybir.AxisListType.X
NT = 4
NEG = -1e30
D = 1024
W1 = 384
W2 = 640
N_IN1 = 4096
N_IN2 = 2840
RING = 8
NWS = 4
PACE = (0.0, 1.0)
MOD_AT = 26
LEAD = (0.0, 0.0)


class Eng:

    def __init__(self, e):
        self.e = e
        self.seen = {}
        self.clock = 0.0

    def wait(self, toks):
        for sem, val in toks:
            if self.seen.get(id(sem), 0) < val:
                self.seen[id(sem)] = val
                self.e.wait_ge(sem, val)


class Forecast:

    def __init__(self):
        self.at = {}

    def of(self, toks):
        return max([self.at.get((id(s), v), 0.0) for s, v in toks] + [0.0])

    def put(self, tok, t):
        self.at[(id(tok[0]), tok[1])] = t
        return tok


class Queue:

    def __init__(self, eng, sem, cast, chain=True, weave=None):
        self.eng, self.sem, self.n, self.chain = eng, sem, 0, chain
        self.cast, self.weave = cast, weave

    def __call__(self, fn, *toks, d=0.5):
        if self.chain and self.n:
            toks = toks + ((self.sem, self.n),)
        toks = [t for t in toks if t]
        ready = self.cast.of(toks)
        if self.weave:
            self.weave(self.eng, ready)
        self.eng.wait(toks)
        self.n += 1
        fn(self.eng.e).then_inc(self.sem, 1)
        self.eng.clock = max(self.eng.clock, ready) + d
        return self.cast.put((self.sem, self.n), self.eng.clock + 0.15)

    def now(self):
        return (self.sem, self.n) if self.n else None


class Dma:

    def __init__(self, eng, sem, cast, wire):
        self.eng, self.sem, self.n = eng, sem, 0
        self.cast, self.wire = cast, wire

    def __call__(self, fn, *toks, d=0.3):
        toks = [t for t in toks if t]
        self.eng.wait(toks)
        self.n += 16
        fn(self.eng.e).then_inc(self.sem, 16)
        self.eng.clock = max(self.eng.clock, self.cast.of(toks)) + 0.1
        self.wire[0] = max(self.wire[0], self.eng.clock) + d
        return self.cast.put((self.sem, self.n), self.wire[0] + 2.0)


def build(nc, A, out, act_counts):
    ctx = ExitStack()
    with ctx:
        total = [0]

        def sb(name, shape, dt=F32):
            return ctx.enter_context(nc.sbuf_tensor(name, shape, dt))

        nsem = [0]

        def sem(name):
            nsem[0] += 1
            return ctx.enter_context(nc.semaphore(name))

        ps_all = ctx.enter_context(nc.psum_tensor("ps", [128, 8, 512], F32))
        PS = [ps_all[:, i, :] for i in range(8)]
        PA = PS[6:8]

        vec, sca, ten, pool, syn = Eng(nc.vector), Eng(nc.scalar), Eng(nc.tensor), Eng(nc.gpsimd), Eng(nc.sync)
        cast = Forecast()
        wire = [0.0]
        pend = [None, None]

        def g_next():
            pend[1] = next(pend[0], None)
            if pend[1] is None:
                pend[0] = None

        def g_start():
            if pend[0] is None:
                return 1e30
            eng, when = pend[1]
            if eng is None and len(when) == 3:
                return 0.0 if when[0:2] in gate_done else 1e30
            if eng is None:
                return 0.0 if when in idx_done else 1e30
            return max(eng.clock, when)

        def weave(eng, ready):
            while g_start() + LEAD[part_at[0] // 4] <= max(eng.clock, ready):
                g_next()

        paced = [0.0]

        def pace(rows):
            paced[0] = max(paced[0], r_n[0] - 2.0) + rows
            while r_n[0] < paced[0] and g_start() < 1e30:
                g_next()

        def gathered(n):
            while gather_done[n] is None:
                assert g_start() < 1e30
                g_next()
            return gather_done[n]

        V = Queue(vec, sem("vA"), cast, weave=weave)
        S = Queue(sca, sem("sA"), cast, weave=weave)
        T = Queue(ten, sem("tA"), cast, chain=False, weave=weave)
        VG = Queue(vec, sem("vG"), cast, chain=False)
        SG = Queue(sca, sem("sG"), cast, chain=False)
        TG = Queue(ten, sem("tG"), cast, chain=False)

        def dma(name):
            return Dma(syn, sem("d_" + name), cast, wire)

        ident = sb("ident", [128, 128])
        shm = sb("shm", [128, 4, 128])
        iot = sb("iot", [128, 16])
        rmask = sb("rmask", [128, 1])
        hres = sb("hres", [128, NT, D])
        ring = sb("ring", [128, RING, D])
        xn = sb("xn", [128, 2, D])
        idx = sb("idx", [128, 2, 128], U32)
        gate = sb("gate", [128, 2, 128])
        aw = sb("aw", [128, 2, 128])
        diag = sb("diag", [128, 4, 128])
        wsl = sb("wsl", [128, NWS, 4, 512])
        xr = sb("xr", [128, D])
        fin = sb("fin", [128, D])
        gt2 = sb("gt2", [128, D])
        finr = sb("finr", [128, D])
        xT = sb("xT", [128, 8, 128])
        st = sb("st", [128, 8])
        cols = sb("cols", [128, 64])
        skT = sb("skT", [128, 8, 128])
        rowA = sb("rowA", [128, D])
        rowB = sb("rowB", [128, D])
        big = sb("big", [128, 6144 + 384])
        pers = sb("pers", [128, 13312])

        def carve(base, start, *shape, dt=F32):
            n = int(np.prod(shape))
            ap = base[:, start:start + n]
            if dt != F32:
                ap = ap.bitcast(dt)
            if len(shape) == 2:
                ap = ap.rearrange("p (a b) -> p a b", b=shape[1])
            if len(shape) == 3:
                ap = ap.rearrange("p (a b c) -> p a b c", b=shape[1], c=shape[2])
            return ap, start + n

        def bc(ap, shape):
            return ap.broadcast_to(shape)

        L1d = nc.dram_tensor("L1d", [16, 128, W1], F32, kind="Internal").ap()
        L2d = nc.dram_tensor("L2d", [8, 128, W2], F32, kind="Internal").ap()

        modd = nc.dram_tensor("modd", [12, 512], F32, kind="Internal").ap()

        d_c = [dma(f"c{i}") for i in range(40)]
        nload = [0]

        def load(dst, src, *toks):
            q = d_c[nload[0]]
            nload[0] += 1
            return q(lambda e: e.dma_start(dst, src), *toks)

        t_id = load(ident[:, :], A["k_ident"])
        t_x = [load(hres[:, i, :], A["x"][0, 128 * i:128 * i + 128, :]) for i in range(NT)]
        t_cols = load(cols[:, 0:54], A["k_cols"])
        t_shm = load(shm[:, :, :], A["k_shift"])
        t_iot = load(iot[:, :], A["k_iota"])
        t_rm = load(rmask[:, :], A["k_rmask"])
        g1c = cols[:, 0:8]
        qgc, kgc, dcol = cols[:, 8:9], cols[:, 9:10], cols[:, 10:14]
        lnm, ngc, ccol = cols[:, 16:24], cols[:, 24:32], cols[:, 32:40]

        w_dma = [dma(f"w{i}") for i in range(NWS)]
        w_free = [None] * NWS
        w_n = [0]
        w_out = [0]

        def w_load(w, k0, kc, c0, n):
            s = w_n[0] % NWS
            w_n[0] += 1
            w_out[0] += 1
            assert w_out[0] <= NWS
            src = w[k0 * 128:(k0 + kc) * 128, c0:c0 + n].rearrange("(k p) n -> p k n", p=128)
            t = w_dma[s](lambda e: e.dma_start(wsl[:, s, 0:kc, 0:n], src), w_free[s], d=n / 512 * 2.9)
            return s, t

        bank_free = {}
        part_at = [0]

        class Proj:

            def __init__(self, w, nk, blocks):
                self.w, self.nk = w, nk
                self.rows = PACE[part_at[0] // 4]
                self.blocks = blocks
                self.units = [(b, k0) for b in range(len(blocks)) for k0 in range(0, nk, 4)]
                self.at = 0
                self.got = {}

            def ahead(self, n):
                while self.at < len(self.units) and self.at < n:
                    b, k0 = self.units[self.at]
                    c0, w = self.blocks[b]
                    self.got[self.at] = w_load(self.w, k0, 4, c0, w)
                    self.at += 1

            def run(self, lhsT, t_l, evac, banks):
                per = self.nk // 4
                for b, (c0, n) in enumerate(self.blocks):
                    bank = banks[b % len(banks)]
                    for u in range(per):
                        i = b * per + u
                        self.ahead(i + 1)
                        s, t_w = self.got[i]

                        def f(e, s=s, u=u, bank=bank, n=n):
                            for k in range(4):
                                kk = 4 * u + k
                                r = e.matmul(PS[bank][:, 0:n], lhsT(kk), wsl[:, s, k, 0:n],
                                             start=(kk == 0), stop=(kk == self.nk - 1))
                            return r
                        pace(self.rows * n / 512)
                        t_mm = T(f, t_w, t_l, bank_free.get(bank), d=4 * 0.86 * n / 512)
                        w_out[0] -= 1
                        w_free[s] = t_mm
                        self.ahead(i + 1 + NWS)
                        yield 1
                    bank_free[bank] = evac(b, PS[bank], t_mm)
                    yield 1

        def rstd(src, t_src, n, c):
            t = S(lambda e: e.activation(xr[:, 0:n], src, ACT.Square, accum_out=st[:, c:c + 1]), t_src, V.now(), T.now())
            t = V(lambda e: e.tensor_scalar(st[:, c:c + 1], st[:, c:c + 1], 1.0 / n, 1e-6, ALU.mult, ALU.add), t)
            t = V(lambda e: e.reciprocal(st[:, c:c + 1], st[:, c:c + 1]), t)
            return S(lambda e: e.activation(st[:, c:c + 1], st[:, c:c + 1], ACT.Sqrt), t)

        def turn(srcs, t_src, bank, t_bank, rows=128):
            def f(e):
                for j, s in enumerate(srcs):
                    r = e.transpose(PS[bank][:, j * 128:(j + 1) * 128], s, ident[:, :])
                return r
            return T(f, t_src, t_bank, t_id)

        def P3(bank, n=4):
            return PS[bank][:, :].rearrange("p (a b) -> p a b", a=n)

        def turn8(src, t_src, dst, evac, t_dst=None):
            toks = []
            for hh in range(2):
                t = turn([src(4 * hh + j) for j in range(4)], t_src, hh, V.now())
                toks.append(t)
            for hh in range(2):
                t = evac(hh, P3(hh), toks[hh], t_dst)
            return t

        def scale_evac(g):
            def f(hh, ps, t, t_dst):
                return V(lambda e: e.tensor_tensor(xT[:, 4 * hh:4 * hh + 4, :], ps,
                                                   bc(g[:, 4 * hh:4 * hh + 4].unsqueeze(2), [128, 4, 128]),
                                                   ALU.mult), t, t_cols, T.now())
            return f

        half = [None]

        def copy_evac(dst):
            def f(hh, ps, t, t_dst):
                if hh == 0:
                    half[0] = act(dst[:, 0:4, :], ps, ACT.Copy, t, t_dst)
                    return half[0]
                return V(lambda e: e.tensor_copy(dst[:, 4:8, :], ps), t, t_dst, half[0], d=0.65)
            return f

        o = 0
        Ec, o = carve(pers, o, 16, 128)
        Es, o = carve(pers, o, 16, 128)
        bias1, o = carve(pers, o, 16, 256)
        kT1, o = carve(pers, o, 2, 512)
        v1, o = carve(pers, o, 2, 256)
        BT, o = carve(pers, o, 8, 128)
        CT, o = carve(pers, o, 32, 32)
        hst, o = carve(pers, o, 2, 16)
        magc, o = carve(pers, o, 16)
        snk, o = carve(pers, o, 16)
        assert o <= 13312, o

        def size(ap):
            return int(np.prod(ap.shape[1:]))

        def tt(out, a, b, op, *toks):
            return V(lambda e: e.tensor_tensor(out, a, b, op), *toks, d=0.1 + size(out) / 960)

        def ts(out, a, s1, s2, o1, o2, *toks):
            if s2 is None:
                return V(lambda e: e.tensor_scalar(out, a, s1, None, o1), *toks, d=0.1 + size(out) / 960)
            return V(lambda e: e.tensor_scalar(out, a, s1, s2, o1, o2), *toks, d=0.1 + size(out) / 960)

        def act(out, a, f, *toks, **kw):
            return S(lambda e: e.activation(out, a, f, **kw), *toks, d=0.3 + size(out) / 1200)

        t_C = [None]
        t_bias = [None]

        def make_bias(tab, nh, oh, msk, w, Ld, dst, keys, t_dst, base, o0):
            o = o0
            ohb, o = carve(base, o, w)
            mk, o = carve(base, o, w)
            tb, o = carve(base, o, 16)
            lv, o = carve(base, o, w)
            t1 = load(ohb[0:32, :], oh, V.now(), T.now(), S.now())
            t2 = load(mk[0:nh, :], msk)
            t3 = load(tb[0:32, 0:nh], tab)
            a = min(512, w)

            def f(e):
                r = e.matmul(PS[0][0:nh, 0:a], tb[0:32, 0:nh], ohb[0:32, 0:a], start=True, stop=True)
                if w > 512:
                    r = e.matmul(PS[1][0:nh, 0:w - 512], tb[0:32, 0:nh], ohb[0:32, 512:w], start=True, stop=True)
                return r
            t = T(f, t1, t3, V.now())
            t = tt(lv[0:nh, 0:a], PS[0][0:nh, 0:a], mk[0:nh, 0:a], ALU.add, t, t2)
            if w > 512:
                t = tt(lv[0:nh, 512:w], PS[1][0:nh, 0:w - 512], mk[0:nh, 512:w], ALU.add)
            t = load(Ld, bc(lv[0:nh, 0:w].unsqueeze(1), [nh, 128, w]), t)
            src = bass.AP(tensor=Ld.tensor, offset=127, ap=[[w - 1, 128], [128 * w, nh], [1, keys]])
            return load(dst, src, t, t_dst)

        rflat = ring[:, :, :].rearrange("p a b -> p (a b)")

        def setup1():
            o = 0
            prm, o = carve(rflat, o, 4, 16)
            tmp, o = carve(rflat, o, 12, 16)
            craw, o = carve(rflat, o, 32, 32)
            ctm, o = carve(rflat, o, 32, 32)
            ea, o = carve(rflat, o, 16, 64)
            t_p = load(prm[:, :, :], A["k_s5p"])
            t_b = load(BT[:, :, :], A["k_s5b"])
            t_cr = load(craw[:, :, :], A["k_s5c"])
            t_s = load(snk[:, :], A["attn_sinks"].broadcast_to([128, 16]))
            lr, li, ls = prm[:, 0, :], prm[:, 1, :], prm[:, 2, :]
            step, th, w0, w1, w2, w3 = [tmp[:, i, :] for i in range(6)]
            cs, sn, cr, ci, den = [tmp[:, i, :] for i in range(6, 11)]
            t = act(step, ls, ACT.Exp, t_p)
            t = tt(th, li, step, ALU.mult, t)
            t = tt(w0, lr, step, ALU.mult)
            t = act(magc[:, :], w0, ACT.Exp, t)
            C1 = 6.28125
            C2 = float(np.float32(2 * math.pi - C1))
            C3 = 2 * math.pi - C1 - C2
            for dst, turn_ in ((sn, 0.0), (cs, 0.25)):
                ts(w1, th, 1.0 / (2 * math.pi), turn_, ALU.mult, ALU.add)
                ts(w1, w1, 12582912.0, None, ALU.add, None)
                ts(w1, w1, -12582912.0, None, ALU.add, None)
                V(lambda e: e.scalar_tensor_tensor(w2, w1, -C1, th, ALU.mult, ALU.add), t)
                V(lambda e: e.scalar_tensor_tensor(w2, w1, -C2, w2, ALU.mult, ALU.add))
                V(lambda e: e.scalar_tensor_tensor(w2, w1, -C3, w2, ALU.mult, ALU.add))
                if turn_:
                    ts(w2, w2, math.pi / 2, None, ALU.add, None)
                t = ts(w2, w2, 3.1415925, -3.1415925, ALU.min, ALU.max)
                t = act(dst, w2, ACT.Sin, t)
            tt(w0, magc[:, :], cs, ALU.mult, t)
            ts(w0, w0, -1.0, None, ALU.add, None)
            tt(w1, magc[:, :], sn, ALU.mult)
            tt(den, lr, lr, ALU.mult)
            tt(w2, li, li, ALU.mult)
            tt(den, den, w2, ALU.add)
            V(lambda e: e.reciprocal(den, den))
            tt(cr, w0, lr, ALU.mult)
            tt(w2, w1, li, ALU.mult)
            tt(cr, cr, w2, ALU.add)
            tt(cr, cr, den, ALU.mult)
            tt(ci, w1, lr, ALU.mult)
            tt(w2, w0, li, ALU.mult)
            tt(ci, ci, w2, ALU.subtract)
            t = tt(ci, ci, den, ALU.mult)
            yield 1
            crb = bc(cr.unsqueeze(2), [128, 16, 32])
            cib = bc(ci.unsqueeze(2), [128, 16, 32])
            t = tt(CT[:, 0:16, :], craw[:, 0:16, :], crb, ALU.mult, t_cr)
            tt(ctm[:, 0:16, :], craw[:, 16:32, :], cib, ALU.mult)
            tt(CT[:, 0:16, :], CT[:, 0:16, :], ctm[:, 0:16, :], ALU.subtract)
            tt(CT[:, 16:32, :], craw[:, 0:16, :], cib, ALU.mult)
            tt(ctm[:, 0:16, :], craw[:, 16:32, :], crb, ALU.mult)
            tt(CT[:, 16:32, :], CT[:, 16:32, :], ctm[:, 0:16, :], ALU.add)
            ts(CT[:, 16:32, :], CT[:, 16:32, :], -1.0, None, ALU.mult, None)
            V(lambda e: e.tensor_copy(Ec[:, :, 0:1], cs.unsqueeze(2)))
            V(lambda e: e.tensor_copy(Es[:, :, 0:1], sn.unsqueeze(2)))
            n = 1
            while n < 128:
                ac = bc(Ec[:, :, n - 1:n], [128, 16, n])
                as_ = bc(Es[:, :, n - 1:n], [128, 16, n])
                tt(ea[:, :, 0:n], Es[:, :, 0:n], as_, ALU.mult)
                tt(Ec[:, :, n:2 * n], Ec[:, :, 0:n], ac, ALU.mult)
                tt(Ec[:, :, n:2 * n], Ec[:, :, n:2 * n], ea[:, :, 0:n], ALU.subtract)
                tt(ea[:, :, 0:n], Es[:, :, 0:n], ac, ALU.mult)
                tt(Es[:, :, n:2 * n], Ec[:, :, 0:n], as_, ALU.mult)
                tt(Es[:, :, n:2 * n], Es[:, :, n:2 * n], ea[:, :, 0:n], ALU.add)
                n *= 2
                yield 1
            t_C[0] = V(lambda e: e.memset(hst[:, :, :], 0.0), t_b, t_s)
            t_bias[0] = make_bias(A["rel_bias_table"], 16, A["k_oh1"], A["k_mask1"], W1, L1d,
                                  bias1[:, :, :], 256, None, rflat, 3328)


        def both(*gens):
            gens = list(gens)
            while gens:
                for g in list(gens):
                    if next(g, None) is None:
                        gens.remove(g)
                yield 1

        def block1(i, side=None):
            W = A["w_in"][0]
            pin = Proj(W, 8, [(512 * b, 512) for b in range(8)])
            pin.ahead(NWS)
            o = 0
            gt, o = carve(big, o, 2048)
            mix, o = carve(big, o, 1024)
            o0 = o
            uT, o = carve(big, o, 4, 128)
            qs, o = carve(big, o, 1024)
            kk, o = carve(big, o, 256)
            t_r = rstd(hres[:, i, :], t_x[i], D, 0)
            t = ts(xr[:, :], hres[:, i, :], st[:, 0:1], None, ALU.mult, None, t_r)
            t_xT = turn8(lambda k: xr[:, k * 128:(k + 1) * 128], t, xT, scale_evac(g1c))
            yield 1
            bg = [None]
            t_bg = load1(gt, A["b_gate"][0].unsqueeze(0).broadcast_to([128, 2048]), V.now(), S.now(), T.now())
            last = {}

            def evac(b, ps, t):
                if b == 0:
                    r = act(xr[:, 0:512], ps[:, :], ACT.Copy, t)
                elif b < 3:
                    r = act(qs[:, 512 * (b - 1):512 * b], ps[:, :], ACT.Copy, t)
                elif b == 3:
                    act(kk[:, :], ps[:, 0:256], ACT.Copy, t)
                    r = act(v1[:, i % 2, :], ps[:, 256:512], ACT.Copy)
                else:
                    g = gt[:, 512 * (b - 4):512 * (b - 3)]
                    r = tt(g, ps[:, :], g, ALU.add, t, t_bg)
                    act(g, g, ACT.Sigmoid, r)
                last[b] = r
                for _ in range(3):
                    if side:
                        next(side, None)
                return r
            yield from pin.run(lambda k: xT[:, k, :], t_xT, evac, [4, 5])
            for _ in side or ():
                pass
            pg = Proj(A["s5_w_glu"][0], 4, [(0, 512), (512, 512)])
            pg.ahead(2)
            t_gates = S.now()
            t = turn([xr[:, j * 128:(j + 1) * 128] for j in range(4)], last[0], 0, V.now())
            t_uT = V(lambda e: e.tensor_copy(uT[:, :, :], P3(0)), t)
            sq, _ = carve(big, o, 1024)
            q3 = qs.rearrange("p (h d) -> p h d", d=64)
            k3 = kk.rearrange("p (h d) -> p h d", d=64)
            hn = cols2
            t = act(sq[:, :], qs[:, :], ACT.Square, V.now())
            t = V(lambda e: e.tensor_reduce(hn[:, 0:16], sq.rearrange("p (h d) -> p h d", d=64), AXX, ALU.add), t)
            t = act(sq[:, 0:256], kk[:, :], ACT.Square, t)
            V(lambda e: e.tensor_reduce(hn[:, 16:20], sq[:, 0:256].rearrange("p (h d) -> p h d", d=64), AXX, ALU.add), t)
            ts(hn[:, 0:20], hn[:, 0:20], 1.0 / 64, 1e-6, ALU.mult, ALU.add)
            t = V(lambda e: e.reciprocal(hn[:, 0:20], hn[:, 0:20]))
            t = act(hn[:, 0:20], hn[:, 0:20], ACT.Sqrt, t)
            tt(q3, q3, bc(hn[:, 0:16].unsqueeze(2), [128, 16, 64]), ALU.mult, t)
            t = tt(k3, k3, bc(hn[:, 16:20].unsqueeze(2), [128, 4, 64]), ALU.mult)
            yield 1
            q4 = qs.rearrange("p (m a r d) -> p m r a d", m=2, a=2, r=4)
            V(lambda e: e.tensor_copy(sq.rearrange("p (m r a d) -> p m r a d", m=2, r=4, a=2)[:, 0], q4[:, 0]))
            t = V(lambda e: e.tensor_copy(sq.rearrange("p (m r a d) -> p m r a d", m=2, r=4, a=2)[:, 1], q4[:, 1]))
            for hh in range(2):
                t = turn([sq[:, 512 * hh + j * 128:512 * hh + (j + 1) * 128] for j in range(4)], V.now(), hh, V.now())
                t = ts(xT[:, 4 * hh:4 * hh + 4, :], P3(hh), qgc, 0.125, ALU.mult, ALU.mult, t)
            t_qT = t
            t = turn([kk[:, 0:128], kk[:, 128:256]], V.now(), 0, V.now())
            t_kT = ts(kT1[:, :, 128 * i:128 * i + 128], PS[0][:, 0:256].rearrange("p (a b) -> p a b", a=2), kgc,
                      None, ALU.mult, None, t)
            yield 1
            av = xr
            s0 = 128 if i == 0 else 0
            ks = range(s0 // 128, 2)
            mx, nm, sm = cols2[:, 20:36], cols2[:, 36:52], cols2[:, 52:68]
            sc = gt2[:, :].rearrange("p (a b) -> p a b", a=4)
            PT = rowB[:, :].rearrange("p (a b) -> p a b", a=4)
            t_att = [None]

            yield from tops.get(i - 1, ())

            def attention():
                t_p0 = t_p1 = None
                for g in range(4):
                    m, a = g // 2, g % 2
                    hs = slice(4 * g, 4 * g + 4)

                    def f(e):
                        for r in range(4):
                            k0 = 128 * (i - 1) + s0
                            x = e.matmul(PS[r // 2][:, 256 * (r % 2) + s0:256 * (r % 2) + 256],
                                         xT[64 * a:64 * a + 64, 4 * m + r, :],
                                         kT1[64 * a:64 * a + 64, m, k0:128 * (i + 1)], start=True, stop=True)
                        return x
                    t = T(f, t_qT, t_kT, t_p0, t_p1, d=0.8 * len(ks))
                    yield 1
                    for b in range(2):
                        t = tt(sc[:, 2 * b:2 * b + 2, s0:256], PS[b].rearrange("p (a b) -> p a b", a=2)[:, :, s0:256],
                               bias1[:, 4 * g + 2 * b:4 * g + 2 * b + 2, s0:256], ALU.add, t, t_bias[0])
                    V(lambda e: e.tensor_reduce(mx[:, hs], sc[:, :, s0:256], AXX, ALU.max), d=1.1)
                    tt(mx[:, hs], mx[:, hs], snk[:, hs], ALU.max)
                    t = ts(nm[:, hs], mx[:, hs], -1.0, None, ALU.mult, None)
                    yield 1
                    for r in range(4):
                        h = 4 * g + r
                        t = act(sc[:, r, s0:256], sc[:, r, s0:256], ACT.Exp, t, bias=nm[:, h:h + 1],
                                accum_out=sm[:, h:h + 1])
                    yield 1

                    def f(e):
                        for r in range(4):
                            for k in ks:
                                x = e.transpose(PS[r // 2][:, 256 * (r % 2) + 128 * k:256 * (r % 2) + 128 * k + 128],
                                                sc[:, r, 128 * k:128 * k + 128], ident[:, :])
                        return x
                    t = T(f, t, d=0.8 * len(ks))
                    yield 1
                    srcs = [PS[b].rearrange("p (a b) -> p a b", a=2)[:, :, s0:256] for b in range(2)]
                    t_p0 = act(PT[:, 0:2, s0:256], srcs[0], ACT.Copy, t)
                    t_p1 = V(lambda e: e.tensor_copy(PT[:, 2:4, s0:256], srcs[1]), t, d=0.6)
                    yield 1

                    def f(e):
                        for r in range(4):
                            h = 4 * g + r
                            for k in ks:
                                x = e.matmul(PS[4 + h // 8][:, 64 * (h % 8):64 * (h % 8) + 64],
                                             PT[:, r, 128 * k:128 * k + 128],
                                             v1[:, (i + 1 + k) % 2, 64 * g:64 * g + 64],
                                             start=(k == ks[0]), stop=(k == 1))
                        return x
                    t_pv = T(f, t_p0, t_p1, bank_free.get(4), bank_free.get(5), d=0.8 * len(ks))
                    yield 1
                tt(mx, snk[:, :], mx, ALU.subtract)
                t = act(mx, mx, ACT.Exp, V.now())
                yield 1
                tt(sm, sm, mx, ALU.add, t)
                V(lambda e: e.reciprocal(sm, sm))
                for b in range(2):
                    t_att[0] = bank_free[4 + b] = tt(
                        av[:, 512 * b:512 * b + 512].rearrange("p (h d) -> p h d", d=64),
                        PS[4 + b].rearrange("p (h d) -> p h d", d=64),
                        bc(sm[:, 8 * b:8 * b + 8].unsqueeze(2), [128, 8, 64]), ALU.mult, t_pv)

            o = o0 + 512
            b0, o = carve(big, o, 4, 128)
            b1, o = carve(big, o, 4, 128)
            b2, o = carve(big, o, 4, 128)
            b3, _ = carve(fin, 0, 4, 128)
            yT, _ = carve(fin, 512, 4, 128)
            pair = ps_all[:, 2:4, :].rearrange("p b (h z c) -> p z h b c", h=2, z=2)

            def hb(x):
                return x.rearrange("p (h b) c -> p h b c", h=2)

            def states():
                t_y = None
                for c in range(4):
                    t = (t_uT, t_C[0], t_y)
                    for h in range(2):
                        def f(e):
                            for z in range(2):
                                for b in range(2):
                                    j = 2 * h + b
                                    x = e.matmul(PS[2 + b][:, 256 * h + 128 * z:256 * h + 128 * z + 128],
                                                 BT[32 * j:32 * j + 32, 4 * z + c, :], uT[32 * j:32 * j + 32, c, :],
                                                 start=True, stop=True, tile_position=(32 * j, 0))
                            return x
                        t = (T(f, *t, d=0.9),)
                    t = t[0]
                    yield 1
                    ec, es = hb(Ec[:, 4 * c:4 * c + 4, :]), hb(Es[:, 4 * c:4 * c + 4, :])
                    pr, pi = pair[:, 0], pair[:, 1]
                    tt(hb(b0), pr, ec, ALU.mult, t)
                    tt(hb(b1), pi, es, ALU.mult)
                    tt(b0, b0, b1, ALU.add)
                    yield 1
                    tt(hb(b1), pi, ec, ALU.mult)
                    tt(hb(b2), pr, es, ALU.mult)
                    tt(b1, b1, b2, ALU.subtract)
                    yield 1
                    for j in range(4):
                        jj = 4 * c + j
                        for z, bb, dd in ((0, b0, b2), (1, b1, b3)):
                            V(lambda e: e.tensor_tensor_scan(
                                dd[:, j, :], bc(magc[:, jj:jj + 1], [128, 128]), bb[:, j, :], hst[:, z, jj:jj + 1],
                                ALU.mult, ALU.add), d=0.35)
                        if j % 2:
                            yield 1
                    ec, es = Ec[:, 4 * c:4 * c + 4, :], Es[:, 4 * c:4 * c + 4, :]
                    tt(b0, b2, ec, ALU.mult)
                    tt(b1, b3, es, ALU.mult)
                    tt(b0, b0, b1, ALU.subtract)
                    yield 1
                    tt(b1, b3, ec, ALU.mult)
                    tt(b2, b2, es, ALU.mult)
                    tt(b1, b1, b2, ALU.add)
                    V(lambda e: e.tensor_copy(hst[:, 0, 4 * c:4 * c + 4].unsqueeze(2), b0[:, :, 127:128]), d=0.1)
                    t = V(lambda e: e.tensor_copy(hst[:, 1, 4 * c:4 * c + 4].unsqueeze(2), b1[:, :, 127:128]), d=0.1)
                    yield 1

                    def f(e):
                        for j in range(4):
                            for z, bb in ((0, b0), (1, b1)):
                                x = e.matmul(PS[2][32 * j:32 * j + 32, 0:128],
                                             CT[:, 16 * z + 4 * c + j, :], bb[:, j, :], start=(z == 0), stop=(z == 1),
                                             tile_position=(0, 32 * j))
                        return x
                    t = T(f, t, d=1.7)
                    yield 1
                    t_y = V(lambda e: e.scalar_tensor_tensor(yT[:, c, :], uT[:, c, :], dcol[:, c:c + 1],
                                                             PS[2][:, 0:128], ALU.mult, ALU.add), t, t_cols, d=0.25)
                    yield 1
            yield from both(attention(), states())
            t = t_att[0]
            pa = Proj(A["w_attn_branch"][0], 8, [(0, 512), (512, 512)])
            t_xT = turn8(lambda k: av[:, k * 128:(k + 1) * 128], t, xT, copy_evac(xT[:, :, :]), T.now())

            def evac(b, ps, t):
                return tt(mix[:, 512 * b:512 * b + 512], ps[:, :], gt[:, 1024 + 512 * b:1536 + 512 * b], ALU.mult,
                          t, t_gates)
            t_attn_x = t_xT
            t = act(yT, yT, ACT.Gelu, V.now())
            gl = b0

            def evac_glu(b, ps, t):
                if b == 0:
                    return V(lambda e: e.tensor_copy(qa, ps[:, :]), t)
                r = act(qb, ps[:, :], ACT.Sigmoid, t, V.now())
                tt(qa, qa, qb, ALU.mult, r)
                return r
            qa = b0.rearrange("p a b -> p (a b)")
            qb = b1.rearrange("p a b -> p (a b)")
            yield from pg.run(lambda k: yT[:, k, :], t, evac_glu, [4, 5])
            pa.ahead(2)
            yield from pa.run(lambda k: xT[:, k, :], t_attn_x, evac, [4, 5])
            ps_ = Proj(A["w_s5_branch"][0], 4, [(0, 512), (512, 512)])
            ps_.ahead(2)
            t = turn([qa[:, j * 128:(j + 1) * 128] for j in range(4)], V.now(), 0, V.now())
            t = V(lambda e: e.tensor_copy(yT, P3(0)), t)

            def evac_s(b, ps, t):
                g = gt[:, 512 * b:512 * b + 512]
                r = tt(g, ps[:, :], g, ALU.mult, t)
                tt(mix[:, 512 * b:512 * b + 512], mix[:, 512 * b:512 * b + 512], g, ALU.add)
                return r
            yield from ps_.run(lambda k: yT[:, k, :], t, evac_s, [4, 5])
            po = Proj(A["w_out"][0], 8, [(0, 512), (512, 512)])
            po.ahead(NWS)
            t = turn8(lambda k: mix[:, k * 128:(k + 1) * 128], V.now(), xT, copy_evac(xT[:, :, :]), T.now())

            def evac_o(b, ps, t):
                h = hres[:, i, 512 * b:512 * b + 512]
                return tt(h, ps[:, :], h, ALU.add, t)
            yield from po.run(lambda k: xT[:, k, :], t, evac_o, [4, 5])

        d_bg = dma("bg")

        def load1(dst, src, *toks):
            return d_bg(lambda e: e.dma_start(dst, src), *toks)

        cols2 = sb("cols2", [128, 96])

        idx_done = {}
        gate_done = {}
        gather_done = [None] * 8

        t_rows = [None, None]

        tops = {}

        def route(n, t_h):
            i, blk, b = n % 4, n // 4, n % 2
            wq = A["peer_w_query"][0] if blk == 0 else A["peer_wq_2"][0]
            pq = Proj(wq, 8, [(0, 512), (512, 512)])
            pq.ahead(NWS)
            if blk:
                o = 0
                sS, o = carve(big, o, 16, 128)
                halves = [sS[:, 0:8, :], sS[:, 8:16, :]]
                base = big
            else:
                halves = [fin[:, :].rearrange("p (a b) -> p a b", b=128), gt2[:, :].rearrange("p (a b) -> p a b", b=128)]
                base, o = rowB, 0
            s2, o1_ = carve(base, o, 256)
            cand, o1_ = carve(base, o1_, 16, 16)
            oh, o = carve(base, o, 2, 16, 16)
            vals, o = carve(base, o, 2, 16)
            ixu, o = carve(base, o, 2, 16, dt=U32)
            ixf, o = carve(base, o, 2, 16)
            best, o = carve(base, o, 8, 16)
            pos, o = carve(base, o, 16, dt=U32)
            pij, o = carve(base, o, 2, 16, dt=U32)
            pf, o = carve(base, o, 2, 16)
            ee, o = carve(base, o, 2, 16)
            nb, o = carve(base, o, 8)
            zs, o = carve(base, o, 8)
            free = gathered(n - 2) if n >= 2 else ()
            t_r = rstd(hres[:, i, :], t_h, D, 1)
            X = xn[:, b, :]
            t = V(lambda e: e.scalar_tensor_tensor(X, hres[:, i, :], st[:, 1:2], rowA[:, :], ALU.mult, ALU.mult),
                  t_r, t_rows[0], *free)
            if blk:
                t = tt(X, X, rowB[:, :], ALU.add, t_rows[1])
            t = turn8(lambda k: X[:, k * 128:(k + 1) * 128], t, xT, copy_evac(xT[:, :, :]), T.now())
            yield 1

            def evac(bb, ps, t):
                return act(xr[:, 512 * bb:512 * bb + 512], ps[:, :], ACT.Copy, t)
            yield from pq.run(lambda k: xT[:, k, :], t, evac, [4, 5])
            t = turn8(lambda k: xr[:, k * 128:(k + 1) * 128], S.now(), xT, copy_evac(xT[:, :, :]), T.now())
            yield 1
            def f(e):
                for h in range(8):
                    for k in range(2):
                        x = e.matmul(PS[2 * k + h // 4][:, 128 * (h % 4):128 * (h % 4) + 128],
                                     xT[64 * k:64 * k + 64, h, :], skT[64 * k:64 * k + 64, h, :],
                                     start=True, stop=True, tile_position=(64 * k, 0))
                return x
            t2 = T(f, t, t_sk[blk], V.now(), S.now())
            for p in range(4):
                hv_ = halves[p % 2].rearrange("p (h k) c -> p h k c", k=2)
                act(hv_[:, :, p // 2, :], P3(p), ACT.Copy, t2, V.now())
            t = S.now()
            yield 1

            def top16(src, scratch, vd, idd, t=None):
                d = 0.1 + size(src) / 960
                V(lambda e: e.max(vd[:, 0:8], src), t, d=d)
                V(lambda e: e.max_index(idd[:, 0:8], vd[:, 0:8], src), d=d)
                V(lambda e: e.match_replace(scratch, vd[:, 0:8], src, -3.0e38), d=d)
                V(lambda e: e.max(vd[:, 8:16], scratch), d=d)
                V(lambda e: e.max_index(idd[:, 8:16], vd[:, 8:16], scratch), d=d)
            iob = bc(iot[:, :].unsqueeze(1).unsqueeze(1), [128, 2, 16, 16])

            def gates(h, t):
                V(lambda e: e.reciprocal(zs[:, h:h + 1], zs[:, h:h + 1]), t, d=0.1)
                gate_done[n, h] = ts(gate[:, b, 16 * h:16 * h + 16], best[:, h, :], zs[:, h:h + 1], None,
                                     ALU.mult, None)

            def top(t):
                t_e = None
                for h in range(8):
                    for k in range(2):
                        top16(halves[h // 4][:, 2 * (h % 4) + k, :], s2[:, 0:128], vals[:, k, :], ixu[:, k, :], t)
                    V(lambda e: e.tensor_copy(ixf, ixu), d=0.15)
                    tt(cand, bc(vals[:, 0, :].unsqueeze(2), [128, 16, 16]), bc(vals[:, 1, :].unsqueeze(1), [128, 16, 16]),
                       ALU.add)
                    top16(cand.rearrange("p a b -> p (a b)"), s2[:, :], best[:, h, :], pos)
                    yield 1
                    ts(pij[:, 0, :], pos, 4, None, ALU.logical_shift_right, None)
                    ts(pij[:, 1, :], pos, 15, None, ALU.bitwise_and, None)
                    V(lambda e: e.tensor_copy(pf, pij), d=0.15)
                    tt(oh, bc(pf.unsqueeze(3), [128, 2, 16, 16]), iob, ALU.is_equal, t_iot)
                    tt(oh, oh, bc(ixf.unsqueeze(2), [128, 2, 16, 16]), ALU.mult)
                    V(lambda e: e.tensor_reduce(ee, oh, AXX, ALU.add), d=0.65)
                    idx_done[n, h] = V(lambda e: e.scalar_tensor_tensor(
                        idx[:, b, 16 * h:16 * h + 16], ee[:, 0, :], 128.0, ee[:, 1, :], ALU.mult, ALU.add), *free, d=0.15)
                    t_n = ts(nb[:, h:h + 1], best[:, h, 0:1], -1.0, None, ALU.mult, None)
                    if h:
                        gates(h - 1, t_e)
                    t_e = act(best[:, h, :], best[:, h, :], ACT.Exp, t_n, bias=nb[:, h:h + 1], accum_out=zs[:, h:h + 1])
                    yield 1
                gates(7, t_e)
            tops[n] = top(t)

        t_sk = [None, None]
        r_sem = [sem(f"ring{i}") for i in range(RING)]
        r_cnt = [0] * RING
        r_free = [None] * RING
        r_n = [0]

        def fetch(tab, m, e_):
            s = r_n[0] % RING
            r_n[0] += 1
            r_cnt[s] += 16
            n = m // 8
            toks = [x for x in (r_free[s], idx_done[n, m % 8]) if x]
            pool.wait(toks)
            ix = idx[:, n % 2, e_:e_ + 1]
            pool.e.indirect_dma_start(out=ring[:, s, :], out_offset=None, in_=tab,
                                      in_offset=bass.IndirectOffsetOnAxis(ap=ix, axis=0)).then_inc(r_sem[s], 16)
            pool.clock = max(pool.clock, cast.of(toks)) + 1.0
            wire[0] = max(wire[0], pool.clock) + 1.5
            return s, cast.put((r_sem[s], r_cnt[s]), wire[0] + 2.0)

        t_w = {}
        dg_n = [0]
        dg_free = [None] * 4
        acc_free = [None]

        def half_u(m, e_):
            n, g = divmod(m, 8)
            b = n % 2
            tab = A["peer_u"][0] if n < 4 else A["peer_u_2"][0]
            k = 16 * g + e_
            s, t = fetch(tab, m, k)
            yield vec, cast.of([t])
            r_free[s] = VG(lambda e: e.tensor_tensor_reduce(ring[:, s, :], ring[:, s, :], xn[:, b, :], 1.0, 0.0,
                                                            ALU.mult, ALU.add, aw[:, b, k:k + 1]), t,
                           gather_done[n - 2][0] if n >= 2 else None, d=1.2)
            if e_ == 15:
                sl = aw[:, b, 16 * g:16 * g + 16]
                tu = r_free[s]
                yield sca, cast.of([tu])
                t = SG(lambda e: e.activation(sl, sl, ACT.Gelu if n < 4 else ACT.Gelu_apprx_tanh), tu, d=0.4)
                while (n, g) not in gate_done:
                    yield None, (n, g, "gate")
                yield vec, cast.of([t])
                t_w[m] = VG(lambda e: e.tensor_tensor(sl, sl, gate[:, b, 16 * g:16 * g + 16], ALU.mult), t,
                              gate_done[n, g], d=0.2)

        def half_v(m, e_):
            n, g = divmod(m, 8)
            b = n % 2
            tab = A["peer_v"][0] if n < 4 else A["peer_v_2"][0]
            k = 16 * g + e_
            s, t = fetch(tab, m, k)
            q = dg_n[0] % 4
            dg_n[0] += 1
            yield sca, cast.of([x for x in (t_w[m], dg_free[q]) if x])
            t_d = SG(lambda e: e.activation(diag[:, q, :], ident[:, :], ACT.Copy, scale=aw[:, b, k:k + 1]),
                     t_w[m], dg_free[q], t_id, d=0.4)
            yield ten, cast.of([t, t_d])

            def f(e):
                for c in range(2):
                    r = e.matmul(PA[c][:, :], diag[:, q, :], ring[:, s, 512 * c:512 * c + 512],
                                 start=(k == 0), stop=(k == 127))
                return r
            dg_free[q] = r_free[s] = TG(f, t, t_d, acc_free[0] if k == 0 else None, d=1.75)

        t_res = [None] * 4
        out_done = []
        out_dma = [Dma(sca, sem(f"o{i}"), cast, wire) for i in range(4)]

        def finish(n):
            i = n % 4
            t = TG.now()
            if n < 4:
                for c in range(2):
                    h = hres[:, i, 512 * c:512 * c + 512]
                    yield vec, cast.of([t])
                    t = VG(lambda e: e.tensor_tensor(h, PA[c][:, :], h, ALU.add), t, d=0.7)
                t_res[i] = acc_free[0] = t
            else:
                for c in range(2):
                    f = fin[:, 512 * c:512 * c + 512]
                    yield vec, cast.of([t])
                    t = VG(lambda e: e.tensor_tensor(f, PA[c][:, :], gt2[:, 512 * c:512 * c + 512], ALU.mult),
                           t, out_done[-1] if out_done else None, d=0.7)
                acc_free[0] = t
                t = VG(lambda e: e.tensor_tensor(fin[:, :], fin[:, :], hres[:, i, :], ALU.add), t, d=1.2)
                yield sca, cast.of([t])
                t = SG(lambda e: e.activation(hres[:, i, :], fin[:, :], ACT.Square, accum_out=st[:, 2:3]), t, d=1.2)
                yield vec, cast.of([t])
                t = VG(lambda e: e.tensor_scalar(st[:, 2:3], st[:, 2:3], 1.0 / D, 1e-6, ALU.mult, ALU.add), t, d=0.1)
                t = VG(lambda e: e.reciprocal(st[:, 2:3], st[:, 2:3]), t, d=0.1)
                yield sca, cast.of([t])
                t = SG(lambda e: e.activation(st[:, 2:3], st[:, 2:3], ACT.Sqrt), t, d=0.3)
                yield vec, cast.of([t])
                t = VG(lambda e: e.scalar_tensor_tensor(fin[:, :], fin[:, :], st[:, 2:3], finr[:, :], ALU.mult,
                                                        ALU.mult), t, d=1.2)
                yield sca, cast.of([t])
                out_done.append(out_dma[i](lambda e: e.dma_start(out[0, 128 * i:128 * i + 128, :], fin[:, :]), t))

        def gathers():
            yield None, (0, 0)
            for e_ in range(16):
                yield from half_u(0, e_)
            for m in range(64):
                n = m // 8
                go = m + 1 < 64 and divmod(m + 1, 8) in idx_done
                for e_ in range(16):
                    if go:
                        yield from half_u(m + 1, e_)
                    yield from half_v(m, e_)
                if m % 8 == 7:
                    gather_done[n] = (TG.now(), VG.now(), SG.now())
                    yield from finish(n)
                if not go and m + 1 < 64:
                    yield None, divmod(m + 1, 8)
                    for e_ in range(16):
                        yield from half_u(m + 1, e_)

        o = 0
        bias2, o = carve(pers, o, 8, 512)
        w1k, o = carve(pers, o, 32, 64)
        w1v, o = carve(pers, o, 32, 64)
        w2k, o = carve(pers, o, 64)
        w2v, o = carve(pers, o, 64)
        pek, o = carve(pers, o, 32)
        pev, o = carve(pers, o, 32)
        kcT, o = carve(pers, o, 512)
        vcT, o = carve(pers, o, 512)
        ksT, o = carve(pers, o, 2, 512)
        vsn, o = carve(pers, o, 4, 256)
        kcc, o = carve(pers, o, 32)
        hv, o = carve(pers, o, 32)
        zprev, o = carve(pers, o, 512)
        gt1, o = carve(pers, o, 1024)
        g1m, o = carve(pers, o, 8)
        sh1, o = carve(pers, o, 8)
        assert o <= 13312, o
        t_m2 = [None]
        cwd = [None]

        bmd = [dma(f"bm{q}") for q in range(2)]
        bm_n = [0]
        bm_free = [None, None]

        def mod_rows(which, dst, bm, toks):
            modr = modd.rearrange("(a b) c -> a (b c)", b=2)
            for q in which:
                z = bm_n[0] % 2
                bm_n[0] += 1
                t1 = load(dst[q], modr[q:q + 1, :].broadcast_to([128, 1024]), *toks)
                t2 = bmd[z](lambda e: e.dma_start(
                    bm[:, z, :], A["b_mod_2"][0:1, 1024 * q:1024 * q + 1024].broadcast_to([128, 1024])), bm_free[z])
                t_rows[1] = bm_free[z] = tt(dst[q], dst[q], bm[:, z, :], ALU.add, t1, t2)
                yield 1

        def setup2():
            V0, T0, S0 = V.now(), T.now(), S.now()
            t = load(w1k, A["k_w1k"], V0, T0, S0, *mod_out)
            toks = [t]
            toks.append(load(w1v, A["k_w1v"]))
            toks.append(load(w2k, A["k_w2k"]))
            toks.append(load(w2v, A["k_w2v"]))
            toks.append(load(pek, A["k_pek"]))
            toks.append(load(pev, A["k_pev"]))
            toks.append(load(finr[:, :], A["ln_final_g_2"].unsqueeze(0).broadcast_to([128, D])))
            t_lf = load(rowA[:, :], A["ln_ffn_g_2"].broadcast_to([128, D]))
            t_sk[1] = load(skT[:, :, :], A["k_sk2"])
            V(lambda e: e.memset(hv, 0.0), V0, T0, S0)
            o = 0
            rows = {}
            for nm_ in ("sh1", "sc1", "sc2"):
                rows[nm_], o = carve(big, o, 1024)
            bm, o = carve(big, o, 2, 1024)
            dst = {0: rows["sh1"], 1: rows["sc1"], 2: gt1, 4: rows["sc2"]}
            yield from mod_rows((0, 1, 2, 4), dst, bm, (V0, T0, S0) + tuple(mod_out))
            for nm_, d, c0 in (("sh1", sh1, 0), ("sc1", g1m, 8)):
                for k in range(8):
                    V(lambda e, nm_=nm_, d=d, k=k: e.tensor_tensor_reduce(
                        xr[:, 0:128], rows[nm_][:, 128 * k:128 * k + 128], ident[:, :], 1.0, 0.0, ALU.mult, ALU.add,
                        d[:, k:k + 1]), T0, S0, S.now())
            V(lambda e: e.scalar_tensor_tensor(g1m, g1m, 1.0, lnm, ALU.add, ALU.mult))
            t_rows[0] = V(lambda e: e.scalar_tensor_tensor(rowA[:, :], rows["sc2"], 1.0, rowA[:, :], ALU.add, ALU.mult),
                          t_lf)
            yield 1
            t_bias[0] = make_bias(A["rel_table_2"], 8, A["k_oh2"], A["k_mask2"], W2, L2d, bias2, 512, None, big, 0)
            t_m2[0] = toks

        mod_out = []

        def modulation():
            ca = cols2[:, 68:76]
            cb = cols2[:, 76:84]
            t = act(cb, ccol, ACT.Sigmoid, t_cols)
            t = tt(ca, cb, ccol, ALU.mult, t)
            slots = [rflat[:, 6144:8192].rearrange("p (k n) -> p k n", n=512),
                     xn[:, :, :].rearrange("p a b -> p (a b)").rearrange("p (k n) -> p k n", n=512)]
            ld = [Dma(pool, sem(f"mw{q}"), cast, wire) for q in range(2)]
            so = [Dma(sca, sem(f"mo{q}"), cast, wire) for q in range(2)]
            mrow = [finr[0:1, 0:512], finr[0:1, 512:1024]]
            w = A["w_mod_2"][0]
            free, t_o, t_w_ = {}, {}, {}

            def get(u):
                b, k0 = divmod(u, 2)
                src = w[512 * k0:512 * k0 + 512, 512 * b:512 * b + 512].rearrange("(k p) n -> p k n", p=128)
                t_w_[u] = ld[u % 2](lambda e: e.dma_start(slots[u % 2], src), free.get(u - 2), d=2.9)
            for _ in range(MOD_AT):
                yield 1
            get(0)
            get(1)
            for u in range(24):
                b, k0 = divmod(u, 2)

                def f(e):
                    for k in range(4):
                        r = e.matmul(PA[b % 2][0:1, :], ca[:, 4 * k0 + k:4 * k0 + k + 1], slots[u % 2][:, k, :],
                                     start=(k0 + k == 0), stop=(k0 * k == 3))
                    return r
                free[u] = T(f, t_w_[u], t, t_o.get(b - 2), d=3.44)
                if u + 2 < 24:
                    get(u + 2)
                yield 1
                if k0:
                    t_o[b] = act(mrow[b % 2], PA[b % 2][0:1, :], ACT.Copy, free[u], mod_out[b - 2] if b > 1 else None)
                    mod_out.append(so[b % 2](lambda e: e.dma_start(modd[b:b + 1, :], mrow[b % 2]), t_o[b]))
                    yield 1

        def block2(i):
            W = A["w_in_2"][0]
            blocks = [(0, 512), (512, 512), (1024, 280), (1816, 512), (2328, 512), (1304, 512)]
            pin = Proj(W, 8, blocks)
            pin.ahead(NWS)
            o = 0
            o1, o = carve(big, o, 512)
            cm, o = carve(big, o, 512)
            bk, o = carve(big, o, 512)
            q2, o = carve(big, o, 512)
            zz, o = carve(big, o, 512)
            o0 = o
            kwv, o = carve(big, o, 288)
            cw, o = carve(big, o, 3, 512)
            nc_ = 8 * i + 7
            t_cw = load1(cw, A["conv_w_2"][0, :, 0, :].unsqueeze(0).broadcast_to([128, 3, 512]),
                         V.now(), S.now(), T.now())
            t_r = rstd(hres[:, i, :], t_res[i], D, 0)
            t = ts(xr[:, :], hres[:, i, :], st[:, 0:1], None, ALU.mult, None, t_r)

            def ev(hh, ps, t, t_dst):
                for j in range(4):
                    k = 4 * hh + j
                    r = ts(xT[:, k, :], ps[:, j, :], g1m[:, k:k + 1], sh1[:, k:k + 1], ALU.mult, ALU.add, t, T.now())
                return r
            t_xT = turn8(lambda k: xr[:, k * 128:(k + 1) * 128], t, xT, ev)
            yield 1
            gg = cols2[:, 0:24]

            def evac(b, ps, t):
                if b == 0:
                    return V(lambda e: e.tensor_copy(
                        q2.rearrange("p (r g d) -> p g r d", g=2, d=64),
                        ps[:, :].rearrange("p (g r d) -> p g r d", g=2, r=4)), t)
                if b == 1:
                    return act(bk, ps[:, :], ACT.Copy, t)
                if b == 2:
                    act(kwv[:, 0:256], ps[:, 0:256], ACT.Copy, t)
                    return act(gg, ps[:, 256:280], ACT.Sigmoid)
                if b == 3:
                    return V(lambda e: e.tensor_copy(zz, ps[:, :]), t, T.now())
                if b == 4:
                    return tt(zz, zz, ps[:, :], ALU.mult, t)
                return act(cm, ps[:, :], ACT.Copy, t)
            yield from pin.run(lambda k: xT[:, k, :], t_xT, evac, [4, 5])
            t_in = S.now()
            def f(e):
                for sh in range(2):
                    r = e.matmul(PS[sh][:, :], shm[:, sh, :], zz, start=True, stop=(i == 0))
                    if i:
                        r = e.matmul(PS[sh][:, :], shm[:, 2 + sh, :], zprev, start=False, stop=True)
                return r
            t = T(f, V.now(), S.now(), t_shm)
            c1, _ = carve(big, o, 512)
            tt(c1, zz, cw[:, 2, :], ALU.mult, t_cw, T.now())
            V(lambda e: e.tensor_copy(zprev, zz), t)
            tt(zz, PS[0][:, :], cw[:, 1, :], ALU.mult, t)
            tt(c1, c1, zz, ALU.add)
            tt(zz, PS[1][:, :], cw[:, 0, :], ALU.mult)
            tt(c1, c1, zz, ALU.add)
            tt(cm, cm, c1, ALU.mult, t_in)
            yield 1
            t = turn([q2[:, 128 * r:128 * r + 128] for r in range(4)], V.now(), 0, V.now())
            t_qT = ts(xT[:, 0:4, :], P3(0), 0.125, None, ALU.mult, None, t, T.now())
            t = turn([bk[:, 0:128], bk[:, 128:256], bk[:, 256:384], kwv[:, 0:128]], t_in, 1, V.now())
            sl = slice(128 * i, 128 * i + 128)
            V(lambda e: e.tensor_copy(kcT[:, sl], PS[1][:, 0:128]), t)
            V(lambda e: e.tensor_copy(vcT[:, sl], PS[1][:, 128:256]))
            t_kT = V(lambda e: e.tensor_copy(ksT[:, :, sl], PS[1][:, 256:512].rearrange("p (a b) -> p a b", a=2)))
            act(vsn[:, i, 0:128], bk[:, 384:512], ACT.Copy)
            t_vs = act(vsn[:, i, 128:256], kwv[:, 128:256], ACT.Copy)
            yield 1
            n0 = 0 if i == 0 else 8 * i - 1
            nn = nc_ - n0
            o = o0
            blk_, o = carve(big, o, 32, 8)
            hk, o = carve(big, o, 32)
            pc, o = carve(big, o, 8, 32)
            vbd, o = carve(big, o, 2, 256)
            ptc, o = carve(big, o, 2, 128)
            for src, pe_, w1_, w2_, isk in ((kcT, pek, w1k, w2k, True), (vcT, pev, w1v, w2v, False)):
                win = bass.AP(tensor=src.tensor, offset=src.offset + 16 * n0,
                              ap=[list(src.ap[0]), [1, 32], [16, nn]])
                t = tt(blk_[:, :, 0:nn], win, bc(pe_.unsqueeze(2), [128, 32, nn]), ALU.add, *t_m2[0], T.now(), S.now())

                def f(e, w1_=w1_):
                    for g in range(2):
                        for j in range(32):
                            r = e.matmul(PS[2][64 * g:64 * g + 64, 0:nn], w1_[64 * g:64 * g + 64, j, :],
                                         blk_[64 * g:64 * g + 64, j, 0:nn], start=(j == 0), stop=(j == 31),
                                         tile_position=(64 * g, 64 * g))
                    return r
                t = T(f, t, V.now())
                d = hk if isk else hv
                d = hk[:, 0:nn] if isk else hv[:, n0:nc_]
                t = act(d, PS[2][:, 0:nn], ACT.Gelu_apprx_tanh, t, T.now(), V.now())
                if isk:
                    def f(e):
                        for g in range(2):
                            r = e.matmul(PS[3][64 * g:64 * g + 64, 0:nn], w2k[64 * g:64 * g + 64, :],
                                         hk[64 * g:64 * g + 64, 0:nn], start=True, stop=True,
                                         tile_position=(64 * g, 64 * g))
                        return r
                    t = T(f, t, V.now())
                    t_kc = V(lambda e: e.tensor_copy(kcc[:, n0:nc_], PS[3][:, 0:nn]), t)
                else:
                    hv4 = cols2[:, 24:28]

                    def f(e):
                        for g in range(2):
                            for r_ in range(4):
                                r = e.matmul(PS[2 + g][32 * r_:32 * r_ + 32, 128:192],
                                             hv[64 * g:64 * g + 64, :], w2v[64 * g:64 * g + 64, :],
                                             start=True, stop=True, tile_position=(64 * g, 32 * r_))
                        return r
                    t = T(f, t, V.now())
                    V(lambda e: e.memset(vbd, 0.0), T.now())
                    for g in range(2):
                        for r_ in range(4):
                            t = V(lambda e, g=g, r_=r_: e.tensor_copy(
                                vbd[32 * r_:32 * r_ + 32, g, 64 * r_:64 * r_ + 64],
                                PS[2 + g][32 * r_:32 * r_ + 32, 128:192]), t)
                    t_vc = t
                yield 1
            sm = cols2[:, 28:52]
            mx = cols2[:, 52:60]
            def f(e):
                for h in range(8):
                    g, r_ = h // 4, h % 4
                    r = e.matmul(PS[2 + g][:, 32 * r_:32 * r_ + nc_], xT[64 * g:64 * g + 64, r_, :],
                                 kcc[64 * g:64 * g + 64, 0:nc_], start=True, stop=True, tile_position=(64 * g, 0))
                return r
            t = T(f, t_qT, t_kc, V.now())
            V(lambda e: e.memset(pc, 0.0), T.now())
            u0 = 415 - 128 * i
            pcv = pc[:, :, 0:nc_]
            for g in range(2):
                bcm = bass.AP(tensor=bias2.tensor, offset=bias2.offset + u0 + 2048 * g,
                              ap=[list(bias2.ap[0]), [512, 4], [16, nc_]])
                tt(pcv[:, 4 * g:4 * g + 4, :], PS[2 + g][:, 0:128].rearrange("p (a b) -> p a b", a=4)[:, :, 0:nc_],
                   bcm, ALU.add, t, t_bias[0])
            V(lambda e: e.tensor_reduce(mx, pcv, AXX, ALU.max))
            t = tt(pcv, pcv, bc(mx.unsqueeze(2), [128, 8, nc_]), ALU.subtract)
            t = act(pcv, pcv, ACT.Exp, t)
            V(lambda e: e.tensor_reduce(sm[:, 0:8], pcv, AXX, ALU.add), t)
            if i == 0:
                ts(pcv, pcv, rmask[:, 0:1], None, ALU.mult, None, t_rm)
            t = turn([pc.rearrange("p a b -> p (a b)")[:, 128 * g:128 * g + 128] for g in range(2)], V.now(), 3, V.now())
            t = V(lambda e: e.tensor_copy(ptc, PS[3][:, 0:256].rearrange("p (a b) -> p a b", a=2)), t)

            def f(e):
                for g in range(2):
                    r = e.matmul(PS[2][:, 256 * g:256 * g + 256], ptc[:, g, :], vbd[:, g, :], start=True, stop=True)
                return r
            t_oc = T(f, t, t_vc, V.now())
            V(lambda e: e.reciprocal(sm[:, 0:8], sm[:, 0:8]))
            g3 = gg.rearrange("p (h c) -> p h c", c=3)
            tt(sm[:, 0:8], sm[:, 0:8], g3[:, :, 0], ALU.mult, t_in)
            o3 = o1.rearrange("p (h d) -> p h d", d=64)
            tt(o3, PS[2][:, :].rearrange("p (h d) -> p h d", d=64), bc(sm[:, 0:8].unsqueeze(2), [128, 8, 64]),
               ALU.mult, t_oc)
            yield 1
            o = o0
            sc, o = carve(big, o, 2, 512)
            PT, o = carve(big, o, 2, 512)
            tmp, o = carve(big, o, 512)
            assert o <= 6528, o
            Wk = 128 * (i + 1)
            sca.wait([V.now()])
            nm = cols2[:, 60:76]
            t_pvs = [None, None]

            def heads(hb, br):
                t_b = t_t = None
                for h in range(hb, 8, 2):
                    g, r_, c = h // 4, h % 4, 8 * br + h

                    def f(e):
                        return e.matmul(PS[hb][:, 0:Wk], xT[64 * g:64 * g + 64, r_, :],
                                        ksT[64 * g:64 * g + 64, br, 0:Wk], start=True, stop=True,
                                        tile_position=(64 * g, 0))
                    t = T(f, t_qT, t_kT, t_first, t_b, d=0.22 * (i + 1))
                    yield 1
                    t_b = tt(sc[:, hb, 0:Wk], PS[hb][:, 0:Wk], bias2[:, h, 384 - 128 * i:512], ALU.add, t, t_bias[0])
                    V(lambda e: e.tensor_reduce(nm[:, c:c + 1], sc[:, hb, 0:Wk], AXX, ALU.max), d=0.1 + Wk / 960)
                    t = ts(nm[:, c:c + 1], nm[:, c:c + 1], -1.0, None, ALU.mult, None)
                    yield 1
                    t = act(sc[:, hb, 0:Wk], sc[:, hb, 0:Wk], ACT.Exp, t, bias=nm[:, c:c + 1],
                            accum_out=sm[:, 8 + c:9 + c])
                    yield 1
                    t = turn([sc[:, hb, 128 * k:128 * k + 128] for k in range(i + 1)], t, 2 + hb, t_t)
                    yield 1
                    if hb:
                        t = t_t = V(lambda e: e.tensor_copy(PT[:, hb, 0:Wk], PS[2 + hb][:, 0:Wk]), t, d=0.1 + Wk / 960)
                    else:
                        t = t_t = act(PT[:, hb, 0:Wk], PS[2 + hb][:, 0:Wk], ACT.Copy, t)
                    yield 1

                    def f(e):
                        for k in range(i + 1):
                            r = e.matmul(PS[4 + br][:, 64 * h:64 * h + 64], PT[:, hb, 128 * k:128 * k + 128],
                                         vsn[:, k, 128 * br + 64 * g:128 * br + 64 * g + 64],
                                         start=(k == 0), stop=(k == i))
                        return r
                    t_pvs[hb] = T(f, t, t_vs, bank_free.get(4 + br), d=0.22 * (i + 1))
                    yield 1
            for br in range(2):
                t_first = V.now()
                yield from both(heads(0, br), heads(1, br))
                V(lambda e: e.reciprocal(sm[:, 8 + 8 * br:16 + 8 * br], sm[:, 8 + 8 * br:16 + 8 * br]), S.now())
                tt(sm[:, 8 + 8 * br:16 + 8 * br], sm[:, 8 + 8 * br:16 + 8 * br], g3[:, :, 1 + br], ALU.mult)
                t3 = tmp.rearrange("p (h d) -> p h d", d=64)
                bank_free[4 + br] = tt(t3, PS[4 + br].rearrange("p (h d) -> p h d", d=64),
                                       bc(sm[:, 8 + 8 * br:16 + 8 * br].unsqueeze(2), [128, 8, 64]), ALU.mult, *t_pvs)
                tt(o1, o1, tmp, ALU.add)
            po = Proj(A["w_out_2"][0], 8, [(0, 512), (512, 512)])
            po.ahead(NWS)
            t = rstd(o1, V.now(), 512, 3)
            t = ts(xr[:, 0:512], o1, st[:, 3:4], None, ALU.mult, None, t)
            t = act(xr[:, 512:1024], cm, ACT.Square, t, T.now(), accum_out=st[:, 4:5])
            ts(st[:, 4:5], st[:, 4:5], 1.0 / 512, 1e-6, ALU.mult, ALU.add, t)
            t = V(lambda e: e.reciprocal(st[:, 4:5], st[:, 4:5]))
            t = act(st[:, 4:5], st[:, 4:5], ACT.Sqrt, t)
            t = ts(xr[:, 512:1024], cm, st[:, 4:5], None, ALU.mult, None, t)
            t = turn8(lambda k: xr[:, k * 128:(k + 1) * 128], t, xT, scale_evac(ngc))
            yield 1

            def evac_o(b, ps, t):
                h = hres[:, i, 512 * b:512 * b + 512]
                r = tt(xr[:, 512 * b:512 * b + 512], ps[:, :], gt1[:, 512 * b:512 * b + 512], ALU.mult, t, T.now())
                tt(h, h, xr[:, 512 * b:512 * b + 512], ALU.add)
                return r
            yield from po.run(lambda k: xT[:, k, :], t, evac_o, [4, 5])

        t_sk[0] = load(skT[:, :, :], A["k_sk1"])
        t_rows[0] = load(rowA[:, :], A["ln2_g"].broadcast_to([128, D]))

        def part(n):
            if n < 4:
                b = block1(n, None if n else setup1())
                yield from both(tops[n - 1] if n else modulation(), b)
                if n == 0:
                    r_free[:] = [T.now()] * RING
                    pool.wait([V.now()])
                    acc_free[0] = S.now()
            else:
                def second():
                    if n == 4:
                        yield from setup2()
                    gathered(n - 4)
                    while t_res[n - 4] is None:
                        g_next()
                    yield from block2(n - 4)
                if n == 4:
                    yield from both(tops[3], second())
                    yield from mod_rows((3, 5), {3: rowB[:, :], 5: gt2[:, :]}, carve(big, 0, 2, 1024)[0],
                                        (V.now(), S.now(), T.now()))
                else:
                    yield from second()
            yield from route(n, V.now())
            if n >= 4:
                yield from tops[n]

        pend[0] = gathers()
        g_next()
        for n in range(8):
            part_at[0] = n
            for _ in part(n):
                pass
        while pend[0] is not None:
            g_next()
        sca.wait(out_done)
        syn.wait(out_done)


def _bucket(dist):
    d = np.maximum(dist, 1).astype(np.float32)
    large = 16 + (np.log(d / 16) / math.log(8) * 16).astype(np.int32)
    return np.where(dist < 16, np.maximum(dist, 0), np.minimum(large, 31))


def _constants():
    c = {"k_ident": np.eye(128, dtype=np.float32)}
    sh = np.zeros((128, 4, 128), np.float32)
    for t in range(128):
        for k, back in enumerate((1, 2)):
            if t >= back:
                sh[t - back, k, t] = 1
            else:
                sh[128 + t - back, 2 + k, t] = 1
    c["k_shift"] = sh
    c["k_iota"] = np.tile(np.arange(16, dtype=np.float32), (128, 1))
    c["k_rmask"] = (np.arange(128) >= 31).astype(np.float32)[:, None]
    for nm, w, nh, top, lim in (("1", W1, 16, 255, 128), ("2", W2, 8, 511, 512)):
        dist = top - np.arange(w)
        ok = (dist >= 0) & (dist < lim)
        oh = np.zeros((32, w), np.float32)
        oh[_bucket(dist)[ok], np.arange(w)[ok]] = 1
        c["k_oh" + nm] = oh
        c["k_mask" + nm] = np.tile(np.where(ok, 0, NEG).astype(np.float32), (nh, 1))
    return c


def kernel(**inputs):
    import concourse.bacc as _bacc
    from concourse.bass_utils import run_bass_kernel_spmd as _run

    nc = _bacc.Bacc("TRN2", target_bir_lowering=False, num_devices=1)
    I = {k: np.asarray(v) for k, v in inputs.items()}
    arr = _constants()
    for k in ("x", "w_in", "b_gate", "s5_w_glu", "w_s5_branch", "rel_bias_table", "attn_sinks", "w_attn_branch",
              "w_out", "ln2_g", "peer_w_query", "peer_u", "peer_v", "ln_ffn_g_2", "w_mod_2", "b_mod_2", "w_in_2",
              "conv_w_2", "w_out_2", "peer_wq_2", "peer_u_2", "peer_v_2", "rel_table_2", "ln_final_g_2"):
        arr[k] = I[k]

    def col(v):
        return v.reshape(-1, 128).T
    cols = np.zeros((128, 54), np.float32)
    cols[:, 0:8] = col(I["ln1_g"][0])
    cols[:, 8] = np.tile(I["q_norm_g"][0], 2)
    cols[:, 9] = np.tile(I["k_norm_g"][0], 2)
    cols[:, 10:14] = col(I["s5_d"][0].reshape(512))
    cols[:, 16:24] = col(I["ln_mix_g_2"][0])
    cols[:, 24:28] = col(I["norm_attn_g_2"][0])
    cols[:, 28:32] = col(I["norm_conv_g_2"][0])
    cols[:, 32:40] = col(I["c_2"][0])
    arr["k_cols"] = cols
    p = np.zeros((128, 4, 16), np.float32)
    p[:, 0] = I["s5_lambda_re"][0].reshape(16, 128).T
    p[:, 1] = I["s5_lambda_im"][0].reshape(16, 128).T
    p[:, 2] = np.repeat(I["s5_log_step"][0], 64).reshape(16, 128).T
    arr["k_s5p"] = p
    bt = np.zeros((4, 2, 16, 2, 4, 2, 64), np.float32)
    for z, k in enumerate(("s5_b_re", "s5_b_im")):
        b = I[k][0].reshape(4, 4, 2, 64, 16)
        for g in range(2):
            bt[:, g, :, z, :, g, :] = b[:, :, g].transpose(1, 3, 0, 2)
    arr["k_s5b"] = bt.reshape(128, 8, 128)
    ct = np.zeros((2, 64, 2, 16, 2, 16), np.float32)
    for z, k in enumerate(("s5_c_re", "s5_c_im")):
        b = I[k][0].reshape(16, 2, 16, 64)
        for g in range(2):
            ct[g, :, z, :, g, :] = b[:, g].transpose(2, 0, 1)
    arr["k_s5c"] = ct.reshape(128, 32, 32)
    for nm, k in (("k_sk1", "peer_sub_keys"), ("k_sk2", "peer_keys_2")):
        arr[nm] = I[k][0].transpose(1, 3, 0, 2).reshape(128, 8, 128)
    for nm, k in (("k_w1k", "cmp_wk1_2"), ("k_w1v", "cmp_wv1_2")):
        w = I[k][0].reshape(32, 64, 64).transpose(1, 0, 2)
        arr[nm] = np.concatenate([w, w], 0)
    for nm, k in (("k_w2k", "cmp_wk2_2"), ("k_w2v", "cmp_wv2_2")):
        arr[nm] = np.concatenate([I[k][0]] * 2, 0)
    for nm, k in (("k_pek", "cmp_pe_k_2"), ("k_pev", "cmp_pe_v_2")):
        arr[nm] = np.concatenate([I[k][0].T] * 2, 0)
    A, maps = {}, {}
    for k, a in arr.items():
        a = np.ascontiguousarray(a)
        maps["in_" + k] = a
        A[k] = nc.dram_tensor("in_" + k, a.shape, mybir.dt.from_np(a.dtype), kind="ExternalInput").ap()
    out = nc.dram_tensor("out_0", (1, 512, D), F32, kind="ExternalOutput").ap()
    build(nc, A, out, None)
    r = _run(nc, [maps], core_ids=[0])
    return r.results[0]["out_0"]
```
